# Optimizing a Trainium2 kernel written in Bass

```python
import jax, jax.numpy as jnp
from jax import lax
import numpy as np

D_MODEL = 2048
BATCH = 1
SEQ = 256
DEPTH = 1

PLE_DIM = 256
A_HEADS = 16
A_KV_GROUPS = 4
A_REP = A_HEADS // A_KV_GROUPS
HEAD_DIM = 64
A_WIDTH = A_HEADS * HEAD_DIM
A_KV_WIDTH = A_KV_GROUPS * HEAD_DIM
CMP_LEN = 32
CMP_STRIDE = 16
CMP_RATIO = CMP_LEN // CMP_STRIDE
SEL_BLOCK = 64
SEL_TOP_N = 16
WINDOW = 512
Q_BLOCK = 128
FORCE_BONUS = 1000.0
B_WIDTH = D_MODEL // 2
B_GROUPS = 8
B_GROUP_DIM = B_WIDTH // B_GROUPS
B_CHUNK = 128
N_BRANCHES = 2
NEG = -1e30
EPS = 1e-6

IN_SPLITS = [A_WIDTH,
             6 * A_KV_WIDTH,
             3 * A_HEADS,
             A_WIDTH,
             2 * B_WIDTH,
             B_WIDTH,
             N_BRANCHES * D_MODEL]
IN_WIDTH = int(sum(IN_SPLITS))
SPLIT_IDX = [int(c) for c in np.cumsum(IN_SPLITS)[:-1]]


def rms_norm(x, g):
    xf = x.astype(jnp.float32)
    y = xf * lax.rsqrt(jnp.mean(xf * xf, axis=-1, keepdims=True) + EPS)
    return (y * g.astype(jnp.float32)).astype(x.dtype)

def layer_norm(x, g, b):
    xf = x.astype(jnp.float32)
    mu = jnp.mean(xf, axis=-1, keepdims=True)
    xc = xf - mu
    y = xc * lax.rsqrt(jnp.mean(xc * xc, axis=-1, keepdims=True) + EPS)
    return (y * g.astype(jnp.float32) + b.astype(jnp.float32)).astype(x.dtype)

def alibi_slopes():
    h = np.arange(1, A_HEADS + 1, dtype=np.float32)
    s = np.power(np.float32(2.0), -8.0 * h / A_HEADS).astype(np.float32)
    return jnp.asarray(s.reshape(A_KV_GROUPS, A_REP))

def compress(kv, pe, w1, w2):
    b, s, g, d = kv.shape
    ch = kv.reshape(b, s // CMP_STRIDE, CMP_STRIDE, g, d)
    nc = s // CMP_STRIDE - CMP_RATIO + 1
    blocks = jnp.concatenate([ch[:, r:nc + r] for r in range(CMP_RATIO)], axis=2)
    blocks = blocks + pe[None, None, :, None, :]
    hid = jax.nn.silu(jnp.einsum('bnlgd,lde->bnge', blocks, w1))
    return jnp.einsum('bnge,ef->bngf', hid, w2)

def nsa_attention(q, k_c, v_c, k_s, v_s, k_w, v_w, gate_logits,
                  pe_k, w1_k, w2_k, pe_v, w1_v, w2_v):
    b, s = q.shape[:2]
    q = q.reshape(b, s, A_KV_GROUPS, A_REP, HEAD_DIM)
    kc = compress(k_c, pe_k, w1_k, w2_k)
    vc = compress(v_c, pe_v, w1_v, w2_v)
    nc = kc.shape[1]
    c_end = jnp.arange(nc, dtype=jnp.int32) * CMP_STRIDE + (CMP_LEN - 1)
    ns = s // SEL_BLOCK
    n_top = min(SEL_TOP_N, ns)
    ci = np.arange(nc)[:, None]
    sj = np.arange(ns)[None, :]
    overlap = jnp.asarray(((CMP_STRIDE * ci < SEL_BLOCK * sj + SEL_BLOCK) &
                           (CMP_STRIDE * ci + CMP_LEN > SEL_BLOCK * sj)).astype(np.float32))
    kb = k_s.reshape(b, ns, SEL_BLOCK, A_KV_GROUPS, HEAD_DIM).transpose(0, 3, 1, 2, 4)
    vb = v_s.reshape(b, ns, SEL_BLOCK, A_KV_GROUPS, HEAD_DIM).transpose(0, 3, 1, 2, 4)
    kw = jnp.pad(k_w, ((0, 0), (WINDOW, 0), (0, 0), (0, 0)))
    vw = jnp.pad(v_w, ((0, 0), (WINDOW, 0), (0, 0), (0, 0)))
    slopes = alibi_slopes()
    gates = jax.nn.sigmoid(gate_logits.astype(jnp.float32)).reshape(b, s, 3, A_KV_GROUPS, A_REP)
    scale = HEAD_DIM ** -0.5
    gather = jax.vmap(jax.vmap(lambda blk, ix: blk[ix]))
    sel_off = jnp.arange(SEL_BLOCK, dtype=jnp.int32)
    win_off = jnp.arange(WINDOW + Q_BLOCK, dtype=jnp.int32)
    blk_ids = jnp.arange(ns, dtype=jnp.int32)

    def block_fn(i):
        q0 = i * Q_BLOCK
        qb = lax.dynamic_slice_in_dim(q, q0, Q_BLOCK, axis=1)
        gb = lax.dynamic_slice_in_dim(gates, q0, Q_BLOCK, axis=1)
        t = q0 + jnp.arange(Q_BLOCK, dtype=jnp.int32)
        dc = t[:, None] - c_end[None, :]
        vc_mask = dc >= 0
        sc = jnp.einsum('bqgrd,bngd->bgrqn', qb, kc).astype(jnp.float32) * scale
        sc = jnp.where(vc_mask, sc - slopes[:, :, None, None] * dc.astype(jnp.float32), NEG)
        p_c = jax.nn.softmax(sc, axis=-1) * vc_mask
        o_c = jnp.einsum('bgrqn,bngd->bqgrd', p_c.astype(vc.dtype), vc)
        imp = jnp.einsum('bgrqn,nj->bgqj', p_c, overlap)
        cur = t // SEL_BLOCK
        forced = ((blk_ids[None, :] == 0) | (blk_ids[None, :] == cur[:, None]) |
                  (blk_ids[None, :] == cur[:, None] - 1))
        causal = blk_ids[None, :] * SEL_BLOCK <= t[:, None]
        score = jnp.where(causal, imp + jnp.where(forced, FORCE_BONUS, 0.0), -1.0)
        _, idx = lax.top_k(score, n_top)
        ks = gather(kb, idx)
        vs = gather(vb, idx)
        pos = idx[..., None] * SEL_BLOCK + sel_off
        ds = (t[None, None, :, None, None] - pos)[:, :, None]
        ss = jnp.einsum('bqgrd,bgqnkd->bgrqnk', qb, ks).astype(jnp.float32) * scale
        ss = jnp.where(ds >= 0, ss - slopes[None, :, :, None, None, None] * ds.astype(jnp.float32), NEG)
        p_s = jax.nn.softmax(ss.reshape(b, A_KV_GROUPS, A_REP, Q_BLOCK, n_top * SEL_BLOCK), axis=-1)
        p_s = p_s.reshape(b, A_KV_GROUPS, A_REP, Q_BLOCK, n_top, SEL_BLOCK)
        o_s = jnp.einsum('bgrqnk,bgqnkd->bqgrd', p_s.astype(vs.dtype), vs)
        kwb = lax.dynamic_slice_in_dim(kw, q0, WINDOW + Q_BLOCK, axis=1)
        vwb = lax.dynamic_slice_in_dim(vw, q0, WINDOW + Q_BLOCK, axis=1)
        kp = q0 - WINDOW + win_off
        dw = t[:, None] - kp[None, :]
        vw_mask = (dw >= 0) & (dw < WINDOW) & (kp[None, :] >= 0)
        sw = jnp.einsum('bqgrd,bkgd->bgrqk', qb, kwb).astype(jnp.float32) * scale
        sw = jnp.where(vw_mask, sw - slopes[:, :, None, None] * dw.astype(jnp.float32), NEG)
        p_w = jax.nn.softmax(sw, axis=-1)
        o_w = jnp.einsum('bgrqk,bkgd->bqgrd', p_w.astype(vwb.dtype), vwb)
        o = (gb[:, :, 0, :, :, None] * o_c + gb[:, :, 1, :, :, None] * o_s +
             gb[:, :, 2, :, :, None] * o_w)
        return o.astype(q.dtype)

    out = lax.map(block_fn, jnp.arange(s // Q_BLOCK, dtype=jnp.int32))
    return out.transpose(1, 0, 2, 3, 4, 5).reshape(b, s, A_WIDTH)

def spatial_gating(uv, ln_g, ln_b, w_s, b_s):
    uv = jax.nn.gelu(uv)
    u, v = jnp.split(uv, 2, axis=-1)
    v = layer_norm(v, ln_g, ln_b)
    b, s, _ = v.shape
    v = v.reshape(b, s // B_CHUNK, B_CHUNK, B_GROUPS, B_GROUP_DIM)
    tril = jnp.tril(jnp.ones((B_CHUNK, B_CHUNK), dtype=w_s.dtype))
    sv = jnp.einsum('gts,bcsgd->bctgd', w_s * tril, v) + b_s.T[None, None, :, :, None]
    return u * sv.reshape(b, s, B_WIDTH)

def first_inputs(seed: int = 0) -> dict:
    key = jax.random.key(seed)
    ks = jax.random.split(key, 24)
    f32 = jnp.float32
    nrm = lambda k, shape, sc: jax.random.normal(k, shape, f32) * sc
    L = DEPTH
    return {
        "x": nrm(ks[0], (BATCH, SEQ, D_MODEL), 1.0),
        "p": nrm(ks[1], (DEPTH, BATCH, SEQ, PLE_DIM), 1.0),
        "norm_g": 1.0 + nrm(ks[2], (L, D_MODEL), 0.05),
        "w_in": nrm(ks[3], (L, D_MODEL, IN_WIDTH), D_MODEL ** -0.5),
        "cmp_pe_k": nrm(ks[4], (L, CMP_LEN, HEAD_DIM), 0.1),
        "cmp_w1_k": nrm(ks[5], (L, CMP_LEN, HEAD_DIM, HEAD_DIM), (CMP_LEN * HEAD_DIM) ** -0.5),
        "cmp_w2_k": nrm(ks[6], (L, HEAD_DIM, HEAD_DIM), HEAD_DIM ** -0.5),
        "cmp_pe_v": nrm(ks[7], (L, CMP_LEN, HEAD_DIM), 0.1),
        "cmp_w1_v": nrm(ks[8], (L, CMP_LEN, HEAD_DIM, HEAD_DIM), (CMP_LEN * HEAD_DIM) ** -0.5),
        "cmp_w2_v": nrm(ks[9], (L, HEAD_DIM, HEAD_DIM), HEAD_DIM ** -0.5),
        "ln_v_g": 1.0 + nrm(ks[10], (L, B_WIDTH), 0.05),
        "ln_v_b": nrm(ks[11], (L, B_WIDTH), 0.02),
        "sgu_w": nrm(ks[12], (L, B_GROUPS, B_CHUNK, B_CHUNK), B_CHUNK ** -0.5),
        "sgu_b": 1.0 + nrm(ks[13], (L, B_GROUPS, B_CHUNK), 0.05),
        "w_up_a": nrm(ks[14], (L, A_WIDTH, D_MODEL), A_WIDTH ** -0.5),
        "w_up_b": nrm(ks[15], (L, B_WIDTH, D_MODEL), B_WIDTH ** -0.5),
        "w_out": nrm(ks[16], (L, D_MODEL, D_MODEL), D_MODEL ** -0.5),
        "w_ple": nrm(ks[17], (L, PLE_DIM, D_MODEL), PLE_DIM ** -0.5),
        "w_ple_gate": nrm(ks[18], (L, D_MODEL, D_MODEL), D_MODEL ** -0.5),
        "final_g": 1.0 + nrm(ks[19], (D_MODEL,), 0.05),
    }

def first_block(x, p, norm_g, w_in, cmp_pe_k, cmp_w1_k, cmp_w2_k, cmp_pe_v, cmp_w1_v, cmp_w2_v,
              ln_v_g, ln_v_b, sgu_w, sgu_b, w_up_a, w_up_b, w_out, w_ple, w_ple_gate, final_g):
    b, s, _ = x.shape
    for l in range(DEPTH):
        h = rms_norm(x, norm_g[l])
        proj = h @ w_in[l]
        q, kv, g_logits, z_a, uv, z_b, merge_logits = jnp.split(proj, SPLIT_IDX, axis=-1)
        k_c, v_c, k_s, v_s, k_w, v_w = [t.reshape(b, s, A_KV_GROUPS, HEAD_DIM)
                                        for t in jnp.split(kv, 6, axis=-1)]
        o_a = nsa_attention(q, k_c, v_c, k_s, v_s, k_w, v_w, g_logits,
                            cmp_pe_k[l], cmp_w1_k[l], cmp_w2_k[l],
                            cmp_pe_v[l], cmp_w1_v[l], cmp_w2_v[l]) * jax.nn.silu(z_a)
        o_b = spatial_gating(uv, ln_v_g[l], ln_v_b[l], sgu_w[l], sgu_b[l]) * jax.nn.silu(z_b)
        g_a, g_b = jnp.split(jax.nn.sigmoid(merge_logits), 2, axis=-1)
        merged = g_a * (o_a @ w_up_a[l]) + g_b * (o_b @ w_up_b[l])
        x = x + merged @ w_out[l]
        x = x + jax.nn.sigmoid(x @ w_ple_gate[l]) * (p[l] @ w_ple[l])
    return rms_norm(x, final_g)


POOL_WIDTH = D_MODEL // 2
POOL_WINDOWS = (2, 4, 8, 16)
POOL_GROUP = POOL_WIDTH // len(POOL_WINDOWS)
LRU_WIDTH = D_MODEL // 2
LRU_HEADS = 8
LRU_HEAD_DIM = LRU_WIDTH // LRU_HEADS
CONV_WIDTH = 4
LRU_C = 8.0
MIX_WIDTH = POOL_WIDTH + LRU_WIDTH
IN_PROJ_WIDTH = POOL_WIDTH + 2 * LRU_WIDTH
PEER_HEADS = 8
PEER_N_KEYS = 128
PEER_N_EXPERTS = PEER_N_KEYS * PEER_N_KEYS
PEER_D_KEY = 256
PEER_HALF = PEER_D_KEY // 2
PEER_TOPK = 16
PEER_CHUNK = 128


def rmsnorm(x, g):
    xf = x.astype(jnp.float32)
    y = xf * lax.rsqrt(jnp.mean(xf * xf, axis=-1, keepdims=True) + EPS)
    return (y * g.astype(jnp.float32)).astype(x.dtype)

def pool_mixer(u, pool_w, pool_b, pool_scale):
    B, S, _ = u.shape
    uf = u.astype(jnp.float32).reshape(B, S, len(POOL_WINDOWS), POOL_GROUP)
    csum = jnp.cumsum(uf, axis=1)
    pos = jnp.arange(1, S + 1, dtype=jnp.float32)[None, :, None]
    outs = []
    for g, w in enumerate(POOL_WINDOWS):
        c = csum[:, :, g]
        c_prev = jnp.pad(c, ((0, 0), (w, 0), (0, 0)))[:, :S]
        mean = (c - c_prev) / jnp.minimum(pos, float(w))
        outs.append(mean - uf[:, :, g])
    d = jnp.stack(outs, axis=2).astype(u.dtype)
    y = jnp.einsum('bsgi,gij->bsgj', d, pool_w) + pool_b
    return y.reshape(B, S, POOL_WIDTH) * pool_scale

def _lru_combine(left, right):
    a1, b1 = left
    a2, b2 = right
    return a1 * a2, a2 * b1 + b2

def rg_lru_mixer(xb, gate, conv_w, conv_b, gate_a_w, gate_a_b, gate_x_w, gate_x_b, lru_lambda):
    B, S, _ = xb.shape
    xp = jnp.pad(xb, ((0, 0), (CONV_WIDTH - 1, 0), (0, 0)))
    xc = conv_b + xp[:, 0:S] * conv_w[0]
    for k in range(1, CONV_WIDTH):
        xc = xc + xp[:, k:k + S] * conv_w[k]
    xh = xc.reshape(B, S, LRU_HEADS, LRU_HEAD_DIM)
    r = jax.nn.sigmoid(jnp.einsum('bshi,hij->bshj', xh, gate_a_w) + gate_a_b).reshape(B, S, LRU_WIDTH)
    i = jax.nn.sigmoid(jnp.einsum('bshi,hij->bshj', xh, gate_x_w) + gate_x_b).reshape(B, S, LRU_WIDTH)
    log_a = (LRU_C * r.astype(jnp.float32)) * jax.nn.log_sigmoid(lru_lambda.astype(jnp.float32))
    a = jnp.exp(log_a)
    mult = jnp.sqrt(-jnp.expm1(2.0 * log_a))
    b = mult * (i * xc).astype(jnp.float32)
    _, h = lax.associative_scan(_lru_combine, (a, b), axis=1)
    return h.astype(xb.dtype) * jax.nn.gelu(gate)

def peer_ffn(z, peer_wq, keys1, keys2, peer_u, peer_v):
    B, S, D = z.shape
    zt = z.reshape(-1, PEER_CHUNK, D)
    k1 = keys1.astype(jnp.float32)
    k2 = keys2.astype(jnp.float32)

    def chunk(zc):
        q = (zc @ peer_wq).astype(jnp.float32).reshape(PEER_CHUNK, PEER_HEADS, 2, PEER_HALF)
        s1 = jnp.einsum('chd,hkd->chk', q[:, :, 0], k1)
        s2 = jnp.einsum('chd,hkd->chk', q[:, :, 1], k2)
        v1, i1 = lax.top_k(s1, PEER_TOPK)
        v2, i2 = lax.top_k(s2, PEER_TOPK)
        cand = (v1[..., :, None] + v2[..., None, :]).reshape(PEER_CHUNK, PEER_HEADS, PEER_TOPK * PEER_TOPK)
        cand_idx = (i1[..., :, None] * PEER_N_KEYS + i2[..., None, :]).reshape(PEER_CHUNK, PEER_HEADS, PEER_TOPK * PEER_TOPK)
        top_s, top_pos = lax.top_k(cand, PEER_TOPK)
        expert = jnp.take_along_axis(cand_idx, top_pos, axis=-1)
        gate = jax.nn.softmax(top_s, axis=-1)
        u = jnp.take(peer_u, expert, axis=0)
        act = jax.nn.gelu(jnp.einsum('chkd,cd->chk', u, zc))
        v = jnp.take(peer_v, expert, axis=0)
        w = (gate * act.astype(jnp.float32)).astype(zc.dtype)
        return jnp.einsum('chk,chkd->cd', w, v).astype(zc.dtype)

    return lax.map(chunk, zt).reshape(B, S, D)

def second_inputs(seed: int = 0) -> dict:
    key = jax.random.key(seed)
    ks = jax.random.split(key, 24)
    L = DEPTH
    f32 = jnp.float32

    def nrm(k, shape, scale):
        return jax.random.normal(k, shape, f32) * scale

    a0 = jax.random.uniform(ks[12], (L, LRU_WIDTH), f32, 0.9, 0.999) ** (1.0 / LRU_C)
    lru_lambda = jnp.log(a0) - jnp.log1p(-a0)
    return {
        "x": nrm(ks[0], (BATCH, SEQ, D_MODEL), 1.0),
        "norm1_g": 1.0 + nrm(ks[1], (L, D_MODEL), 0.02),
        "w_in": nrm(ks[2], (L, D_MODEL, IN_PROJ_WIDTH), D_MODEL ** -0.5),
        "pool_w": nrm(ks[3], (L, len(POOL_WINDOWS), POOL_GROUP, POOL_GROUP), POOL_GROUP ** -0.5),
        "pool_b": nrm(ks[4], (L, len(POOL_WINDOWS), POOL_GROUP), 0.01),
        "pool_scale": 1.0 + nrm(ks[5], (L, POOL_WIDTH), 0.02),
        "conv_w": nrm(ks[6], (L, CONV_WIDTH, LRU_WIDTH), CONV_WIDTH ** -0.5),
        "conv_b": nrm(ks[7], (L, LRU_WIDTH), 0.01),
        "gate_a_w": nrm(ks[8], (L, LRU_HEADS, LRU_HEAD_DIM, LRU_HEAD_DIM), LRU_HEAD_DIM ** -0.5),
        "gate_a_b": nrm(ks[9], (L, LRU_HEADS, LRU_HEAD_DIM), 0.01),
        "gate_x_w": nrm(ks[10], (L, LRU_HEADS, LRU_HEAD_DIM, LRU_HEAD_DIM), LRU_HEAD_DIM ** -0.5),
        "gate_x_b": nrm(ks[11], (L, LRU_HEADS, LRU_HEAD_DIM), 0.01),
        "lru_lambda": lru_lambda,
        "w_out": nrm(ks[13], (L, MIX_WIDTH, D_MODEL), MIX_WIDTH ** -0.5),
        "norm2_g": 1.0 + nrm(ks[14], (L, D_MODEL), 0.02),
        "peer_wq": nrm(ks[15], (L, D_MODEL, PEER_HEADS * PEER_D_KEY), D_MODEL ** -0.5),
        "peer_keys1": nrm(ks[16], (L, PEER_HEADS, PEER_N_KEYS, PEER_HALF), PEER_HALF ** -0.5),
        "peer_keys2": nrm(ks[17], (L, PEER_HEADS, PEER_N_KEYS, PEER_HALF), PEER_HALF ** -0.5),
        "peer_u": nrm(ks[18], (L, PEER_N_EXPERTS, D_MODEL), D_MODEL ** -0.5),
        "peer_v": nrm(ks[19], (L, PEER_N_EXPERTS, D_MODEL), PEER_HEADS ** -0.5),
        "norm_f_g": 1.0 + nrm(ks[20], (D_MODEL,), 0.02),
    }

def second_block(x, norm1_g, w_in, pool_w, pool_b, pool_scale, conv_w, conv_b, gate_a_w, gate_a_b,
              gate_x_w, gate_x_b, lru_lambda, w_out, norm2_g, peer_wq, peer_keys1, peer_keys2,
              peer_u, peer_v, norm_f_g):
    h = x
    for l in range(DEPTH):
        z = rmsnorm(h, norm1_g[l])
        proj = z @ w_in[l]
        u_pool = proj[..., :POOL_WIDTH]
        x_lru = proj[..., POOL_WIDTH:POOL_WIDTH + LRU_WIDTH]
        g_lru = proj[..., POOL_WIDTH + LRU_WIDTH:]
        y_pool = pool_mixer(u_pool, pool_w[l], pool_b[l], pool_scale[l])
        y_lru = rg_lru_mixer(x_lru, g_lru, conv_w[l], conv_b[l], gate_a_w[l], gate_a_b[l],
                             gate_x_w[l], gate_x_b[l], lru_lambda[l])
        y = jnp.concatenate([y_pool, y_lru], axis=-1)
        h = h + y @ w_out[l]
        h = h + peer_ffn(rmsnorm(h, norm2_g[l]), peer_wq[l], peer_keys1[l], peer_keys2[l],
                         peer_u[l], peer_v[l])
    return rmsnorm(h, norm_f_g)


def setup_inputs(seed=0):
    out = dict(first_inputs(seed))
    for name, value in second_inputs(seed + 1).items():
        if name != "x":
            out[name + "_2"] = value
    return out


def reference(
    x, p, norm_g, w_in, cmp_pe_k, cmp_w1_k, cmp_w2_k, cmp_pe_v, cmp_w1_v, cmp_w2_v, ln_v_g,
    ln_v_b, sgu_w, sgu_b, w_up_a, w_up_b, w_out, w_ple, w_ple_gate, final_g, norm1_g_2, w_in_2,
    pool_w_2, pool_b_2, pool_scale_2, conv_w_2, conv_b_2, gate_a_w_2, gate_a_b_2, gate_x_w_2,
    gate_x_b_2, lru_lambda_2, w_out_2, norm2_g_2, peer_wq_2, peer_keys1_2, peer_keys2_2,
    peer_u_2, peer_v_2, norm_f_g_2,
):
    x = first_block(
        x, p, norm_g, w_in, cmp_pe_k, cmp_w1_k, cmp_w2_k, cmp_pe_v, cmp_w1_v, cmp_w2_v, ln_v_g,
        ln_v_b, sgu_w, sgu_b, w_up_a, w_up_b, w_out, w_ple, w_ple_gate, final_g,
    )
    return second_block(
        x, norm1_g_2, w_in_2, pool_w_2, pool_b_2, pool_scale_2, conv_w_2, conv_b_2, gate_a_w_2,
        gate_a_b_2, gate_x_w_2, gate_x_b_2, lru_lambda_2, w_out_2, norm2_g_2, peer_wq_2,
        peer_keys1_2, peer_keys2_2, peer_u_2, peer_v_2, norm_f_g_2,
    )


_drawn_inputs = setup_inputs


def setup_inputs(seed=0):
    import zlib

    import numpy as np

    out = dict(_drawn_inputs(seed))
    spreads = {}
    factors = {'cmp_pe_k': 8.0,
     'cmp_w1_k': 2.703,
     'cmp_w2_k': 2.749,
     'cmp_pe_v': 3.517,
     'ln_v_g': 4.116,
     'ln_v_b': 25.263,
     'sgu_b': 3.284,
     'norm1_g_2': 2.744,
     'pool_b_2': 13.698,
     'pool_scale_2': 9.995,
     'gate_a_b_2': 64.0,
     'gate_x_b_2': 53.425,
     'norm_f_g_2': 21.89,
     'conv_b_2': 6.515,
     'norm2_g_2': 24.775}
    for name, (base, spread) in spreads.items():
        noise = np.random.default_rng([zlib.crc32(name.encode()), seed]).standard_normal(out[name].shape)
        drawn = base * np.exp(spread * noise) if base else spread * noise
        out[name] = __import__('jax').numpy.asarray(drawn.astype(out[name].dtype))
    for name, factor in factors.items():
        out[name] = (out[name] * factor).astype(out[name].dtype)
    return out
```

```python
from contextlib import ExitStack

import numpy as np

import concourse.bass as bass
from concourse import mybir

P = 128
TOK = 256
HALVES = TOK // P
D = 2048
KT = D // P
HEADS, GROUPS, HD = 16, 4, 64
REP = HEADS // GROUPS
A_WIDTH = HEADS * HD
B_WIDTH = D // 2
BT = B_WIDTH // P
CMP_LEN, CMP_STRIDE = 32, 16
NC_BLOCKS = TOK // CMP_STRIDE - CMP_LEN // CMP_STRIDE + 1
NCP = 16
PLE = 256
LRU_C = 8.0
CONV = 4
WINDOWS = (2, 4, 8, 16)
PAD = 16
PEER_HEADS, KEYS, TOPK = 8, 128, 16
EPS = 1e-6
MASKED = -1e30
LOWEST = -3.0e38
GELU_C = 0.044715
GELU_S = float(np.sqrt(2.0 / np.pi))

COL_Q = 0
COL_KV = COL_Q + A_WIDTH
COL_GL = COL_KV + 6 * GROUPS * HD
COL_ZA = COL_GL + 3 * HEADS
COL_U = COL_ZA + A_WIDTH
COL_V = COL_U + B_WIDTH
COL_ZB = COL_V + B_WIDTH
COL_MERGE = COL_ZB + B_WIDTH

PANEL = 2 * P
SLOTS = 4
SECTIONS = {
    "q": (4, 4, 1), "kv": (6, 6, 1), "gl": (1, 1, 1), "main": (32, 8, 1), "up": (8, 4, 2),
    "out": (8, 4, 1), "ple": (8, 4, 2), "in2": (12, 4, 1), "out2": (8, 4, 1), "wq": (8, 4, 1),
}


def section_starts():
    start, counts, at = 0, [0] * SLOTS, {}
    for name, (panels, _, dmas) in SECTIONS.items():
        at[name] = (start, list(counts))
        for n in range(start, start + panels):
            counts[n % SLOTS] += 16 * dmas
        start += panels
    return at


STARTS = section_starts()


def panel(section, j, i=0):
    start, counts = STARTS[section]
    _, body, dmas = SECTIONS[section]
    slot, bank = (start + j) % SLOTS, (start + j) % 2
    landed = i * (16 * dmas * (body // SLOTS)) + (counts[slot] + 16 * dmas * (j // SLOTS + 1))
    released = i * (body // 2) + (start + j) // 2
    done = i * body + (start + j + 1)
    reusable = i * body + (start + j + 1 - SLOTS)
    return slot, bank, landed, released, done, reusable


VEC_A = (("norm_g", 16), ("ln_v_g", 8), ("ln_v_b", 8), ("final_g", 16), ("norm1_g_2", 16), ("conv_w_2", 32),
         ("conv_b_2", 8), ("pool_b_2", 8), ("pool_scale_2", 8), ("gate_a_b_2", 8))
VEC_B = (("gate_x_b_2", 8), ("lru_lambda_2", 8), ("cmp_pe_k", 32), ("cmp_pe_v", 32), ("norm2_g_2", 16))


def vec_columns():
    at, col = {}, 0
    for name, rows in VEC_A + VEC_B:
        at[name] = (col, rows)
        col += rows
    return at, col


VEC_AT, VEC_COLS = vec_columns()
VEC_B_ROWS = VEC_COLS - P

ONCE = (
    "x_in", "vec_in", "sgu_in", "sgub_in", "cmp_in", "pnat_in", "xnat_in", "blk2_in", "keys_in", "bc2_in", "bcf_in", "out_done",
    "ident_ready", "ones_ready", "dist_ready", "half_ready", "zero_ready", "w1_zeroed", "pad_zeroed",
    "wt_ready",
    "vec_t", "vecs_ready", "xt_done", "xt_evac_a", "xt_evac_v", "sgu_t", "sgu_t_evac",
    "sq_ready", "ss_done", "rt_ready", "h_ready",
    "kv_evac", "gl_ready", "gl_t", "gates_ready", "vt_done", "vall_ready", "dup_done", "kpad_a", "kpad_v",
    "kab_ready", "hid_done", "hid_tanh", "hid_ready", "kc_done", "kc_ready", "kcdup_done", "kcpad_ready",
    "mean_done", "xc_ready", "vsq_ready", "var_done", "vrt_ready", "y_ready", "yt_done", "vn_ready", "sv_done",
    "oa_ready", "ob_ready", "up_done", "pt_t", "pt_ready", "xt2_done", "xt2_ready", "x2_ready",
    "pool_d", "pool_mm", "pool_y", "xc2_ready", "lam_u", "lam_ready",
    "lam_abs", "gate_mm", "gate_evac", "rates_ready", "mult2_ready", "mult_ready", "lru_y", "h2_ready",
    "keys_t", "keys_evac", "qp_ready", "h2t_done", "hnat_ready", "ssn_ready", "rtn_ready", "znat_ready", "sc_done",
    "sc_evac", "sc_zero", "fin_sq", "fin_rt", "fin_out",
)
LOOPED = (
    "dense_done", "qv_ready", "th_ready", "gin_ready", "s_done", "s_free", "t_ready", "exp_done", "e_ready",
    "pt_done", "pts_ready", "pv_done", "o_free", "top_ready", "ex_done", "idx_ready", "inner_ready",
    "gel_done", "w_ready", "dve_step", "act_step", "pool_step", "tg_looped", "uz_step", "soft_step", "top_step", "gel_step",
)
AHEAD = 4


def build(nc, T, out):
    f32, u32 = mybir.dt.float32, mybir.dt.uint32
    ACT, ALU, AX = mybir.ActivationFunctionType, mybir.AluOpType, mybir.AxisListType
    ctx = ExitStack()
    with ctx:
        def sb(name, shape, dt=f32):
            return ctx.enter_context(nc.sbuf_tensor(name, shape, dt))

        S = {n: ctx.enter_context(nc.semaphore(n)) for n in ONCE + LOOPED}
        w_landed = [ctx.enter_context(nc.semaphore(f"w_landed{s}")) for s in range(SLOTS)]
        bank_free = [ctx.enter_context(nc.semaphore(f"bank_free{b}")) for b in range(2)]
        u_landed = [ctx.enter_context(nc.semaphore(f"u_landed{s}")) for s in range(4)]
        u_free = [ctx.enter_context(nc.semaphore(f"u_free{s}")) for s in range(4)]
        v_landed = [ctx.enter_context(nc.semaphore(f"v_landed{s}")) for s in range(4)]
        v_free = [ctx.enter_context(nc.semaphore(f"v_free{s}")) for s in range(4)]
        diag_ready = [ctx.enter_context(nc.semaphore(f"diag_ready{s}")) for s in range(4)]

        W = sb("W", [P, SLOTS * KT * PANEL])
        RA = sb("RA", [P, 6144])
        RK = sb("RK", [P, 4096])
        RZ = sb("RZ", [P, 16384])
        RG = sb("RG", [P, 4096])

        def view(region, at, *dims):
            n = int(np.prod(dims))
            v = region[:, at:at + n]
            if len(dims) == 1:
                return v
            names = "abcd"[:len(dims)]
            return v.rearrange(f"p ({' '.join(names)}) -> p {' '.join(names)}", **dict(zip(names, dims)))

        ring = view(W, 0, SLOTS, KT, PANEL)
        xnat0 = view(RZ, 0, HALVES, D)
        hT = view(RA, 0, KT, TOK)
        qT = view(RA, 4096, BT, TOK)
        oaT = qT
        kpad = view(RK, 0, 2, 2, GROUPS, TOK)
        sq = view(RK, 0, KT, TOK)
        kvT = view(RZ, 0, 6, 2, TOK)
        kab = view(RZ, 3072, 4, 2, TOK)
        w1bd = view(RZ, 5120, 2, CMP_LEN, P)
        za, uT, vT, zb = (view(RZ, 2048 * n, BT, TOK) for n in range(4))
        obT = vT
        merge = view(RZ, 8192, 32, TOK)
        vall = view(RG, 0, GROUPS, 5, HD)
        sT = view(RG, 1280, 800)
        eT = view(RG, 2080, 800)
        pts = view(RG, 2880, 1024)
        sgub = RG[0:1, 1280:1280 + BT * P]
        sgun = view(RG, 2304, BT, P)
        sguT = sgun
        vsq = view(RK, 0, BT, TOK)
        vn = view(RK, 2048, HALVES, BT, P)
        mergedT = view(RK, 0, KT, TOK)
        xnat1 = view(RA, 0, HALVES, D)
        x1T = view(RZ, 0, KT, TOK)
        x2T = view(RZ, 4096, KT, TOK)
        wple = view(RZ, 8192, SLOTS, 2, PANEL)
        pnat = view(RZ, 10240, HALVES, PLE)
        pT = view(RZ, 10752, 2, TOK)
        z2T = hT
        upad = view(RZ, 8192, BT, PAD + TOK)
        xpad = view(RZ, 10368, BT, 4 + TOK)
        gT = view(RZ, 12448, BT, TOK)
        lruC = view(RZ, 14496, 64)
        xcT = view(RZ, 0, BT, TOK)
        tiT = view(RZ, 2048, BT, TOK)
        sumA = view(RK, 0, BT, PAD + TOK)
        sumB = view(RK, 2176, 6, PAD + TOK)
        dT = view(RA, 4096, BT, TOK)
        trT = view(RK, 0, BT, TOK)
        multT = view(RK, 2048, BT, TOK)
        aT = view(RA, 4096, BT, TOK)
        poolw = view(RG, 0, 4, 2, TOK)
        gaw = view(RG, 2048, BT, P)
        gxw = view(RG, 3072, BT, P)
        yT = hT
        h2T = view(RZ, 0, KT, TOK)
        z3T = hT
        keysn = view(RA, 4096, 2, PEER_HEADS, P)
        keysT = view(RG, 0, 2, PEER_HEADS, KEYS)
        qp = view(RZ, 8192, KT, TOK)
        hnat = view(RZ, 12288, HALVES, D)
        znat = view(RZ, 4096, HALVES, D)
        g2bc = view(RK, 0, D)
        gfbc = view(RK, 2048, D)
        ROWS = HALVES * PEER_HEADS
        scores = view(RA, 0, ROWS + 2, 2, KEYS)
        junk = [view(RG, 2048, D), view(RZ, D, D)]
        ubuf = view(W, 0, 4, D)
        vbuf = view(W, 4 * D, 4, D)
        stage = view(RZ, 0, HALVES, D)

        ident = sb("ident", [P, P])
        identh = sb("identh", [P, P])
        dup = view(RZ, 14080, 2, P)
        ones = sb("ones", [P, P])
        half = sb("half", [P, 2])
        eps = sb("eps", [P, 2])
        dist = sb("dist", [P, 800])
        cmask = sb("cmask", [P, 32])
        slopes = sb("slopes", [P, HEADS])
        slcur = sb("slcur", [P, REP])
        gates = sb("gates", [P, HEADS, 6])
        gcur = sb("gcur", [P, REP, 6])
        vecA = view(RZ, 13312, P)
        vecB = RZ[0:VEC_B_ROWS, 13440:13440 + P]
        glT = RZ[0:3 * HEADS, 13568:13568 + TOK]
        vecs = sb("vecs", [P, VEC_COLS])
        w2bd = view(RZ, 13824, 2, P)
        hid = sb("hid", [P, 2, 2 * NC_BLOCKS])
        hidt = sb("hidt", [P, 2, 2 * NC_BLOCKS])
        kcT = sb("kcT", [P, 2, NCP])
        kcpad = sb("kcpad", [P, 2, GROUPS, NCP])
        qcur = sb("qcur", [P, 2, TOK])
        vcur = sb("vcur", [P, 5, 3 * HD])
        th = sb("th", [P, 2, PANEL * 2])
        gin = sb("gin", [P, PANEL * 2])
        nmx = sb("nmx", [P, 6])
        sums = sb("sums", [P, 6])
        fac = sb("fac", [P, 6])
        rt = sb("rt", [P, TOK])
        rstd = sb("rstd", [P, TOK])
        inv16 = sb("inv16", [P, 4, PAD])
        iota16 = sb("iota16", [P, TOPK])
        row = view(RZ, 8192, 2, KEYS)
        row2 = view(RZ, 8448, 2, KEYS)
        tv = sb("tv", [P, 2, TOPK])
        ti_u = sb("ti_u", [P, 2, TOPK], u32)
        ti_f = sb("ti_f", [P, 2, TOPK])
        cand = view(RZ, 8704, TOPK, TOPK)
        cand2 = view(RZ, 8960, TOPK, TOPK)
        top = sb("top", [P, 2, TOPK])
        pos = sb("pos", [P, TOPK], u32)
        posab = sb("posab", [P, 2, TOPK], u32)
        posf = sb("posf", [P, 2, TOPK])
        pick = sb("pick", [P, 2, TOPK])
        expf = sb("expf", [P, TOPK])
        idx = sb("idx", [P, 2, TOPK], u32)
        nm = sb("nm", [P, 2])
        eg = sb("eg", [P, 2, TOPK])
        es = sb("es", [P, 2])
        er = sb("er", [P, 2])
        act = sb("act", [P, 2, TOPK])
        asq = sb("asq", [P, TOPK])
        ain = sb("ain", [P, 2, TOPK])
        ath = sb("ath", [P, 2, TOPK])
        agx = sb("agx", [P, 2, TOPK])
        wk = sb("wk", [P, 2, TOPK])
        diag = view(RZ, 9216, 4, P)
        ssn = sb("ssn", [P, 2])
        rtn = sb("rtn", [P, 2])
        rsn = sb("rsn", [P, 2])

        PS = ctx.enter_context(nc.psum_tensor("PS", [P, 4096], f32))

        def bank(b, n=1):
            return PS[:, 512 * b:512 * (b + n)]

        def tiles2(b):
            return bank(b).rearrange("p (t n) -> p t n", t=2)

        pS = bank(2, 2)
        pT_ = bank(4, 2)
        pO = bank(6)[:, 0:TOK]

        def vec(name, n=None):
            c, rows = VEC_AT[name]
            return vecs[:, c:c + rows] if n is None else vecs[:, c + n:c + n + 1]

        def dview(a):
            return a.rearrange("(k p) n -> p k n", p=P)

        x_v = T["x"][0].rearrange("(h p) d -> p h d", p=P)
        w_in = dview(T["w_in"][0])
        w_in2 = dview(T["w_in_2"][0])
        up_a, up_b = dview(T["w_up_a"][0]), dview(T["w_up_b"][0])
        w_out, w_gate, w_ple = dview(T["w_out"][0]), dview(T["w_ple_gate"][0]), dview(T["w_ple"][0])
        w_out2, w_q = dview(T["w_out_2"][0]), dview(T["peer_wq_2"][0])
        peer_u, peer_v = T["peer_u_2"][0], T["peer_v_2"][0]

        def vec_rows(name):
            a = T[name]
            if name.startswith("cmp_pe"):
                return a[0]
            a = a if name == "final_g" else a[0]
            if len(a.shape) > 1:
                a = a.rearrange("a b -> (a b)")
            return a.rearrange("(k p) -> k p", p=P)

        block = ctx.enter_context(nc.Block())

        class Line:

            def __init__(self, eng, sem):
                self.eng, self.sem, self.n = eng, sem, 0

            def do(self, ins):
                self.n += 1
                ins.then_inc(self.sem, 1)
                self.eng.wait_ge(self.sem, self.n)

        @block.sync
        def _(sp):
            def load(section, j, i, *copies):
                slot, _, _, _, _, reusable = panel(section, j, i)
                if STARTS[section][0] + j >= SLOTS:
                    sp.wait_ge(S["dense_done"], reusable)
                for dst, src in copies:
                    sp.dma_start(dst(slot), src).then_inc(w_landed[slot], 16)

            def whole(slot):
                return ring[:, slot, :, :]

            for h in range(HALVES):
                sp.dma_start(xnat0[:, h, :], x_v[:, h, :]).then_inc(S["x_in"], 16)
            for j in range(4):
                load("q", j, 0, (whole, w_in[:, :, COL_Q + j * PANEL:COL_Q + (j + 1) * PANEL]))
            for j in range(6):
                load("kv", j, 0, (whole, w_in[:, :, COL_KV + j * PANEL:COL_KV + (j + 1) * PANEL]))
            load("gl", 0, 0, (lambda s: ring[:, s, :, 0:3 * HEADS], w_in[:, :, COL_GL:COL_ZA]))
            with sp.Fori(0, GROUPS) as i:
                for j, col in enumerate((COL_ZA, COL_U, COL_V, COL_ZB)):
                    load("main", j, i, (whole, w_in[:, :, bass.ds(i * PANEL + col, PANEL)]))
                for j in range(4):
                    load("main", 4 + j, i, (whole, w_in[:, :, bass.ds(i * (4 * PANEL) + (COL_MERGE + j * PANEL), PANEL)]))
            sp.wait_ge(S["dense_done"], STARTS["up"][0])
            sp.dma_start(sgun, T["sgu_w"][0].rearrange("g t s -> t g s")).then_inc(S["sgu_in"], 16)
            sp.dma_start(sgub, T["sgu_b"][0].rearrange("g t -> (g t)").unsqueeze(0)).then_inc(S["sgub_in"], 16)
            for h in range(HALVES):
                sp.dma_start(xnat1[:, h, :], x_v[:, h, :]).then_inc(S["xnat_in"], 16)
            with sp.Fori(0, 2) as i:
                for j in range(4):
                    cols = bass.ds(i * (4 * PANEL) + j * PANEL, PANEL)
                    load("up", j, i, (lambda s: ring[:, s, 0:BT, :], up_a[:, :, cols]),
                         (lambda s: ring[:, s, BT:KT, :], up_b[:, :, cols]))
            with sp.Fori(0, 2) as i:
                for j in range(4):
                    load("out", j, i, (whole, w_out[:, :, bass.ds(i * (4 * PANEL) + j * PANEL, PANEL)]))
            sp.wait_ge(S["up_done"], 8)
            sp.dma_start(pnat, T["p"][0][0].rearrange("(h p) d -> p h d", p=P)).then_inc(S["pnat_in"], 16)
            with sp.Fori(0, 2) as i:
                for j in range(4):
                    cols = bass.ds(i * (4 * PANEL) + j * PANEL, PANEL)
                    load("ple", j, i, (whole, w_gate[:, :, cols]), (lambda s: wple[:, s, :, :], w_ple[:, :, cols]))
            sp.dma_start(poolw, T["pool_w_2"][0].rearrange("g (k p) n -> p g k n", p=P)).then_inc(S["blk2_in"], 16)
            sp.dma_start(gaw, T["gate_a_w_2"][0].rearrange("h p n -> p h n")).then_inc(S["blk2_in"], 16)
            sp.dma_start(gxw, T["gate_x_w_2"][0].rearrange("h p n -> p h n")).then_inc(S["blk2_in"], 16)
            for n, col in enumerate((B_WIDTH, 0, 2 * B_WIDTH)):
                for j in range(4):
                    load("in2", j, n, (whole, w_in2[:, :, col + j * PANEL:col + (j + 1) * PANEL]))
            with sp.Fori(0, 2) as i:
                for j in range(4):
                    load("out2", j, i, (whole, w_out2[:, :, bass.ds(i * (4 * PANEL) + j * PANEL, PANEL)]))
            sp.wait_ge(S["lru_y"], 1)
            for s, name in enumerate(("peer_keys1_2", "peer_keys2_2")):
                sp.dma_start(keysn[:, s], T[name][0].rearrange("h k d -> k h d")).then_inc(S["keys_in"], 16)
            with sp.Fori(0, 2) as i:
                for j in range(4):
                    load("wq", j, i, (whole, w_q[:, :, bass.ds(i * (4 * PANEL) + j * PANEL, PANEL)]))
            sp.wait_ge(S["ss_done"], 4)
            sp.dma_start(g2bc, T["norm2_g_2"][0].partition_broadcast(P)).then_inc(S["bc2_in"], 16)
            sp.dma_start(gfbc, T["norm_f_g_2"].partition_broadcast(P)).then_inc(S["bcf_in"], 16)
            out_v = out[0].rearrange("(h p) d -> p h d", p=P)
            for h in range(HALVES):
                sp.wait_ge(S["fin_out"], h + 1)
                sp.dma_start(out_v[:, h, :], stage[:, h, :]).then_inc(S["out_done"], 16)
            sp.wait_ge(S["out_done"], 16 * HALVES)

        @block.gpsimd
        def _(g):
            line = Line(g, S["pool_step"])
            line.do(g.memset(ident[:], 0.0))
            g.affine_select(out=ident[:], in_=ident[:], compare_op=ALU.not_equal, fill=1.0, base=0,
                            pattern=[[-1, P]], channel_multiplier=1).then_inc(S["ident_ready"], 1)
            g.memset(ones[:], 1.0).then_inc(S["ones_ready"], 1)
            g.memset(eps[:, 0:1], EPS).then_inc(S["ones_ready"], 1)
            g.memset(eps[:, 1:2], 4 * EPS).then_inc(S["ones_ready"], 1)
            g.memset(half[:], 0.0).then_inc(S["zero_ready"], 1)
            g.memset(w2bd, 0.0).then_inc(S["zero_ready"], 1)
            g.memset(kcT[:], 0.0).then_inc(S["zero_ready"], 1)
            g.memset(vcur[:], 0.0).then_inc(S["zero_ready"], 1)
            g.memset(vall[:, :, 4, :], 0.0).then_inc(S["zero_ready"], 1)
            g.memset(dup, 0.0).then_inc(S["zero_ready"], 1)
            g.wait_ge(S["zero_ready"], 6)
            for s in range(2):
                v = dup[:, s, :].rearrange("p (a n) -> p a n", a=2)
                line.do(g.affine_select(out=v, in_=v, compare_op=ALU.not_equal, fill=1.0, base=-HD * s,
                                        pattern=[[0, 2], [-1, HD]], channel_multiplier=1))
            for s in range(2):
                line.do(g.memset(half[s * HD:(s + 1) * HD, s:s + 1], 1.0))
            g.sem_inc(S["half_ready"], 2)
            parts = ((0, 2, TOK, 1, -P), (512, 2, P, 1, 0), (768, 1, NCP, CMP_STRIDE, CMP_LEN - 1),
                     (784, 1, NCP, CMP_STRIDE, CMP_LEN - 1 - P))
            for at, reps, n, step, base in parts:
                v = dist[:, at:at + reps * n].rearrange("p (a n) -> p a n", a=reps)
                line.do(g.iota(v, pattern=[[0, reps], [step, n]], base=base, channel_multiplier=-1,
                               allow_small_or_imprecise_dtypes=True))
                line.do(g.affine_select(out=v, in_=v, compare_op=ALU.is_ge, fill=MASKED, base=-base,
                                        pattern=[[0, reps], [-step, n]], channel_multiplier=1))
            line.do(g.memset(cmask[:], 1.0))
            for s, base in enumerate((CMP_LEN - 1, CMP_LEN - 1 - P)):
                v = cmask[:, s * NCP:(s + 1) * NCP]
                line.do(g.affine_select(out=v, in_=v, compare_op=ALU.is_ge, fill=0.0, base=-base,
                                        pattern=[[-CMP_STRIDE, NCP]], channel_multiplier=1))
            for h in range(HEADS):
                line.do(g.memset(slopes[:, h:h + 1], float(np.float32(2.0) ** np.float32(-8.0 * (h + 1) / HEADS))))
            for n in range(4):
                line.do(g.iota(inv16[:, n, :], pattern=[[1, PAD]], base=1, channel_multiplier=0,
                               allow_small_or_imprecise_dtypes=True))
            line.do(g.iota(iota16[:], pattern=[[1, TOPK]], base=0, channel_multiplier=0,
                           allow_small_or_imprecise_dtypes=True))
            line.do(g.memset(identh[:], 0.0))
            g.affine_select(out=identh[:], in_=identh[:], compare_op=ALU.not_equal, fill=0.5, base=0,
                            pattern=[[-1, P]], channel_multiplier=1).then_inc(S["dist_ready"], 1)
            g.wait_ge(S["sgu_t_evac"], 2)
            g.affine_select(out=sguT, in_=sguT, compare_op=ALU.is_ge, fill=0.0, base=0,
                            pattern=[[0, BT], [1, P]], channel_multiplier=-1).then_inc(S["wt_ready"], 1)
            g.wait_ge(S["x2_ready"], 8)
            g.memset(upad[:, :, 0:PAD], 0.0).then_inc(S["pad_zeroed"], 1)
            g.memset(xpad[:, :, 0:4], 0.0).then_inc(S["pad_zeroed"], 1)
            g.wait_ge(S["qp_ready"], 8)
            g.memset(scores[:, ROWS:ROWS + 2], 0.0).then_inc(S["sc_zero"], 1)

            for s in range(4):
                g.sem_inc(u_free[s], 1)
                g.sem_inc(v_free[s], 1)
            for hf in range(HALVES):
                with g.Fori(0, PEER_HEADS // 2) as i:
                    for par in range(2):
                        r = i * 2 + (PEER_HEADS * hf + par)
                        for table, buf, landed, free in ((peer_u, ubuf, u_landed, u_free), (peer_v, vbuf, v_landed, v_free)):
                            for k in range(TOPK):
                                s = k % 4
                                if k == 0:
                                    g.wait_ge(S["idx_ready"], r + 1)
                                g.wait_ge(free[s], r * 4 + (k // 4 + 1))
                                g.nop(nofuse=True)
                                g.indirect_dma_start(
                                    buf[:, s, :], None, table,
                                    bass.IndirectOffsetOnAxis(ap=idx[:, par, k:k + 1], axis=0)).then_inc(landed[s], 16)

        @block.scalar
        def _(a):
            line = Line(a, S["act_step"])
            for buf, group in ((vecA, VEC_A), (vecB, VEC_B)):
                r = 0
                for name, rows in group:
                    src = vec_rows(name)
                    if name.startswith("cmp_pe"):
                        for s in range(2):
                            a.dma_start(buf[r:r + rows, s * HD:(s + 1) * HD], src).then_inc(S["vec_in"], 16)
                    else:
                        a.dma_start(buf[r:r + rows, :], src).then_inc(S["vec_in"], 16)
                    r += rows

            def norm(n, src):
                a.activation(sq, src, ACT.Square).then_inc(S["sq_ready"], 1)
                a.wait_ge(S["ss_done"], n + 1)
                a.activation(rt[:], bank(7)[:, 0:TOK], ACT.Sqrt, scale=1.0 / D, bias=eps[:, 0:1]).then_inc(S["rt_ready"], 1)

            for gi in range(0, 16, 2):
                a.wait_ge(S["xt_done"], gi + 1)
                a.activation(hT[:, gi, :], bank(2 + gi % 6)[:, 0:TOK], ACT.Copy).then_inc(S["xt_evac_a"], 1)
            a.wait_ge(S["xt_evac_v"], 8)
            a.wait_ge(S["xt_evac_a"], 8)
            a.wait_ge(S["ones_ready"], 3)
            norm(0, hT)
            a.wait_ge(S["w1_zeroed"], 1)
            a.wait_ge(S["zero_ready"], 6)
            for s, kind in enumerate("kv"):
                for hf in range(2):
                    rows = slice(HD * hf, HD * (hf + 1))
                    a.dma_start(w1bd[rows, s, :, rows], T[f"cmp_w1_{kind}"][0].rearrange("l d e -> d l e")).then_inc(S["cmp_in"], 16)
                    a.dma_start(w2bd[rows, s, rows], T[f"cmp_w2_{kind}"][0]).then_inc(S["cmp_in"], 16)
            for j in range(4):
                _, b, _, _, done, _ = panel("q", j)
                a.wait_ge(S["dense_done"], done)
                a.activation(qT[:, 2 * j:2 * j + 2, :], tiles2(b), ACT.Copy, scale=HD ** -0.5).then_inc(bank_free[b], 1)
            for j in range(6):
                _, b, _, _, done, _ = panel("kv", j)
                a.wait_ge(S["dense_done"], done)
                line.do(a.activation(kvT[:, j, :, :], tiles2(b), ACT.Copy))
                a.sem_inc(bank_free[b], 1)
                a.sem_inc(S["kv_evac"], 1)
            _, b, _, _, done, _ = panel("gl", 0)
            a.wait_ge(S["dense_done"], done)
            line.do(a.activation(glT, bank(b)[0:3 * HEADS, 0:TOK], ACT.Tanh, scale=0.5))
            a.sem_inc(bank_free[b], 1)
            a.sem_inc(S["gl_ready"], 1)
            for j in range(2):
                a.wait_ge(S["dup_done"], j + 1)
                for par in range(2):
                    a.activation(kpad[:, par, 0, 2 * j:2 * j + 2, :], tiles2(4 + j), ACT.Copy,
                                 scale=half[:, par:par + 1]).then_inc(S["kpad_a"], 1)
            for s in range(2):
                a.wait_ge(S["hid_done"], s + 1)
                a.activation(hidt[:, s, :], bank(2 + s)[:, 0:2 * NC_BLOCKS], ACT.Tanh, scale=0.5).then_inc(S["hid_tanh"], 1)

            with a.Fori(0, GROUPS) as i:
                thr = i * 6
                for j in range(8):
                    _, b, _, _, done, _ = panel("main", j, i)
                    a.wait_ge(S["dense_done"], done)
                    if j in (0, 3):
                        a.activation(th[:, b, :], bank(b), ACT.Tanh, scale=0.5).then_inc(S["th_ready"], 1)
                    elif j in (1, 2):
                        a.activation(th[:, b, :], bank(b), ACT.Square).then_inc(S["th_ready"], 1)
                        a.wait_ge(S["gin_ready"], i * 2 + j)
                        a.activation(th[:, b, :], gin[:], ACT.Tanh, scale=GELU_S * GELU_C).then_inc(S["th_ready"], 1)
                    else:
                        a.activation(merge[:, bass.ds(i * 8 + 2 * (j - 4), 2), :], tiles2(b), ACT.Tanh, scale=0.5)\
                            .then_inc(bank_free[b], 1)
                    if j in (3, 5):
                        a.wait_ge(S["pv_done"], i * 4 + (j - 1 + AHEAD))
                        a.activation(oaT[:, bass.ds(i * 2 + (j - 3) // 2, 1), :], pO.unsqueeze(1), ACT.Copy)\
                            .then_inc(S["o_free"], 1)
                    if 1 <= j <= 4:
                        h = j - 1
                        a.wait_ge(S["pt_done"], i * 4 + (h + 1))
                        a.wait_ge(S["pv_done"], i * 4 + (h + AHEAD))
                        a.activation(pts[:, 0:768], pT_[:, 0:768], ACT.Copy)
                        a.activation(pts[0:NCP, 768:1024], pT_[0:NCP, 768:1024], ACT.Copy).then_inc(S["pts_ready"], 1)
                    if j < 4:
                        a.wait_ge(S["t_ready"], i * 4 + (j + 1))
                        segments = ((0, TOK), (TOK, TOK), (512, P), (640, P), (768, NCP), (784, NCP))
                        for n, (at, size) in enumerate(segments):
                            ins = a.activation(eT[:, at:at + size], sT[:, at:at + size], ACT.Exp, bias=nmx[:, n:n + 1],
                                               accum_out=sums[:, n:n + 1])
                        ins.then_inc(S["exp_done"], 1)

            for b in range(2):
                a.wait_ge(S["sgu_t"], b + 1)
                a.activation(sguT[:, 4 * b:4 * b + 4, :], bank(4 + b).rearrange("p (g n) -> p g n", g=4),
                             ACT.Copy).then_inc(S["sgu_t_evac"], 1)
            a.wait_ge(S["xc_ready"], 1)
            a.activation(vsq, vT, ACT.Square).then_inc(S["vsq_ready"], 1)
            a.wait_ge(S["var_done"], 1)
            a.activation(rt[:], bank(3)[:, 0:TOK], ACT.Sqrt, scale=1.0 / B_WIDTH, bias=eps[:, 1:2]).then_inc(S["vrt_ready"], 1)
            for n in range(4):
                a.wait_ge(S["yt_done"], n + 1)
                a.activation(vn[:, n // 2, 4 * (n % 2):4 * (n % 2) + 4, :], bank(4 + n).rearrange("p (g n) -> p g n", g=4),
                             ACT.Copy).then_inc(S["vn_ready"], 1)
            for n in range(8):
                a.wait_ge(S["xt2_done"], n + 1)
                a.wait_ge(S["ob_ready"], 1)
                a.wait_ge(S["oa_ready"], 1)
                a.activation(x1T[:, 2 * n:2 * n + 2, :], tiles2(4 + n % 4), ACT.Copy).then_inc(S["xt2_ready"], 1)
            a.wait_ge(S["pt_t"], 1)
            a.activation(pT, tiles2(4), ACT.Copy).then_inc(S["pt_ready"], 1)
            with a.Fori(0, 2) as i:
                for j in range(4):
                    _, b, _, _, done, _ = panel("ple", j, i)
                    a.wait_ge(S["dense_done"], done)
                    a.activation(th[:, b, :], bank(b), ACT.Tanh, scale=0.5).then_inc(S["tg_looped"], 1)
            a.wait_ge(S["x2_ready"], 8)
            norm(1, x2T)
            a.wait_ge(S["h_ready"], 2 * KT)
            norm(2, x2T)
            a.wait_ge(S["lam_abs"], 1)
            a.activation(lruC[:, 8:16], lruC[:, 0:8], ACT.Exp, scale=-1.0).then_inc(S["lam_u"], 1)
            a.wait_ge(S["pad_zeroed"], 2)
            for n, (dst, at) in enumerate(((xpad, 4), (upad, PAD))):
                for j in range(4):
                    _, b, _, _, done, _ = panel("in2", j, n)
                    a.wait_ge(S["dense_done"], done)
                    a.activation(dst[:, 2 * j:2 * j + 2, at:at + TOK], tiles2(b), ACT.Copy).then_inc(bank_free[b], 1)
            for j in range(4):
                _, b, _, _, done, _ = panel("in2", j, 2)
                a.wait_ge(S["dense_done"], done)
                a.activation(th[:, b, :], bank(b), ACT.Square).then_inc(S["th_ready"], 1)
                a.wait_ge(S["gin_ready"], 2 * GROUPS + j + 1)
                a.activation(th[:, b, :], gin[:], ACT.Tanh, scale=GELU_S * GELU_C).then_inc(S["th_ready"], 1)
            a.wait_ge(S["lam_ready"], 1)
            a.wait_ge(S["pool_d"], 1)
            for h in range(BT):
                a.wait_ge(S["gate_mm"], h + 1)
                a.activation(trT[:, h, :], bank(2 + h % 4)[:, 0:TOK], ACT.Tanh, scale=0.5, bias=lruC[:, 40 + h:41 + h]).then_inc(S["gate_evac"], 1)
                a.activation(tiT[:, h, :], bank(2 + h % 4)[:, TOK:2 * TOK], ACT.Tanh, scale=0.5, bias=lruC[:, 48 + h:49 + h])\
                    .then_inc(S["gate_evac"], 1)
            a.wait_ge(S["gate_evac"], 2 * BT)
            a.wait_ge(S["pool_mm"], 4)
            for h in range(BT):
                a.activation(aT[:, h, :], trT[:, h, :], ACT.Exp, scale=lruC[:, 24 + h:25 + h], bias=lruC[:, 24 + h:25 + h])
                a.activation(multT[:, h, :], trT[:, h, :], ACT.Tanh, scale=lruC[:, 32 + h:33 + h], bias=lruC[:, 32 + h:33 + h])\
                    .then_inc(S["rates_ready"], 1)
            a.wait_ge(S["mult2_ready"], 1)
            a.activation(multT, multT, ACT.Sqrt).then_inc(S["mult_ready"], 1)
            for n in range(4):
                a.wait_ge(S["keys_t"], n + 1)
                a.activation(keysT[:, n // 2, 4 * (n % 2):4 * (n % 2) + 4, :], bank(2 + n).rearrange("p (g n) -> p g n", g=4),
                             ACT.Copy).then_inc(S["keys_evac"], 1)
            a.wait_ge(S["h2_ready"], 8)
            norm(3, h2T)
            for n in range(8):
                a.wait_ge(S["h2t_done"], n + 1)
                a.activation(hnat[:, n // 4, 512 * (n % 4):512 * (n % 4) + 512], bank(2 + n % 4), ACT.Copy).then_inc(S["hnat_ready"], 1)
            a.wait_ge(S["hnat_ready"], 8)
            for hf in range(HALVES):
                if hf:
                    a.wait_ge(S["ssn_ready"], hf)
                a.activation(junk[0], hnat[:, hf, :], ACT.Square, accum_out=ssn[:, hf:hf + 1]).then_inc(S["ssn_ready"], 1)
            a.wait_ge(S["ssn_ready"], 2)
            a.activation(rtn[:], ssn[:], ACT.Sqrt, scale=1.0 / D, bias=eps[:, 0:1]).then_inc(S["rtn_ready"], 1)
            with a.Fori(0, 2) as i:
                for j in range(4):
                    _, b, _, _, done, _ = panel("wq", j, i)
                    a.wait_ge(S["dense_done"], done)
                    a.activation(qp[:, bass.ds(i * 8 + 2 * j, 2), :], tiles2(b), ACT.Copy).then_inc(bank_free[b], 1)
            a.wait_ge(bank_free[0], STARTS["wq"][0] // 2 + 4)
            a.wait_ge(bank_free[1], STARTS["wq"][0] // 2 + 4)
            a.sem_inc(S["qp_ready"], 8)
            for r in range(ROWS):
                a.wait_ge(S["sc_done"], r + 1)
                a.activation(scores[:, r], bank(2 + r % 4)[:, 0:2 * KEYS].rearrange("p (s k) -> p s k", s=2), ACT.Copy).then_inc(S["sc_evac"], 1)

            def expo(par, count):
                a.wait_ge(S["top_ready"], count)
                a.activation(eg[:, par, :], top[:, par, :], ACT.Exp, bias=nm[:, par:par + 1],
                             accum_out=es[:, par:par + 1]).then_inc(S["ex_done"], 1)

            expo(0, 1)
            expo(1, 2)
            for hf in range(HALVES):
                with a.Fori(0, PEER_HEADS // 2) as i:
                    for par in range(2):
                        r = i * 2 + (PEER_HEADS * hf + par)
                        a.wait_ge(S["inner_ready"], r + 1)
                        a.activation(ath[:, par, :], ain[:, par, :], ACT.Tanh, scale=GELU_S * GELU_C).then_inc(S["gel_done"], 1)
                        a.wait_ge(S["w_ready"], r + 1)
                        for k in range(TOPK):
                            s = k % 4
                            a.wait_ge(v_free[s], r * 4 + (k // 4 + 1))
                            a.activation(diag[:, s, :], identh[:], ACT.Copy, scale=wk[:, par, k:k + 1]).then_inc(diag_ready[s], 1)
                        expo(par, r + 3)
                a.wait_ge(v_free[3], (hf + 1) * PEER_HEADS * 4 + 1)
                if hf:
                    a.wait_ge(S["fin_out"], hf)
                a.activation(stage[:, hf, :], bank(4 * hf, 4), ACT.Square, accum_out=ssn[:, hf:hf + 1]).then_inc(S["fin_sq"], 1)
                a.wait_ge(S["fin_sq"], hf + 1)
                a.activation(rtn[:, hf:hf + 1], ssn[:, hf:hf + 1], ACT.Sqrt, scale=1.0 / D, bias=eps[:, 0:1]).then_inc(S["fin_rt"], 1)

        @block.vector
        def _(v):
            line = Line(v, S["dve_step"])
            do = line.do

            v.wait_ge(S["vec_t"], 1)
            v.tensor_copy(vecs[:], bank(0)[:, 0:VEC_COLS]).then_inc(S["vecs_ready"], 1)
            for gi in range(1, 16, 2):
                v.wait_ge(S["xt_done"], gi + 1)
                v.tensor_copy(hT[:, gi, :], bank(2 + gi % 6)[:, 0:TOK]).then_inc(S["xt_evac_v"], 1)
            v.memset(w1bd, 0.0).then_inc(S["w1_zeroed"], 1)

            def norm(n, dst, src, gain):
                v.wait_ge(S["rt_ready"], n + 1)
                do(v.reciprocal(rstd[:], rt[:]))
                for k in range(KT):
                    v.scalar_tensor_tensor(dst[:, k, :], src[:, k, :], vec(gain, k), rstd[:], op0=ALU.mult, op1=ALU.mult)\
                        .then_inc(S["h_ready"], 1)

            norm(0, hT, hT, "norm_g")

            for s, name in enumerate(("cmp_pe_k", "cmp_pe_v")):
                v.wait_ge(S["kv_evac"], s + 1)
                c, _ = VEC_AT[name]
                for part in range(2):
                    pe = vecs[:, c + part * CMP_STRIDE:c + (part + 1) * CMP_STRIDE]
                    v.tensor_tensor(
                        kab[:, 2 * s + part].rearrange("p t (n l) -> p (t n) l", l=CMP_STRIDE),
                        kvT[:, s].rearrange("p t (n l) -> p (t n) l", l=CMP_STRIDE),
                        pe.unsqueeze(1).to_broadcast([P, 2 * TOK // CMP_STRIDE, CMP_STRIDE]), ALU.add).then_inc(S["kab_ready"], 1)
            for typ in range(2):
                v.wait_ge(S["vt_done"], typ + 1)
                v.tensor_copy(vall[:, :, 2 * typ:2 * typ + 2, :].rearrange("p g s d -> p s g d"),
                              bank(2 + typ).rearrange("p (s g d) -> p s g d", s=2, g=GROUPS)).then_inc(S["vall_ready"], 1)
            v.wait_ge(S["half_ready"], 2)
            for j in range(2):
                v.wait_ge(S["dup_done"], 3 + j)
                for par in range(2):
                    v.tensor_scalar(kpad[:, par, 1, 2 * j:2 * j + 2, :], tiles2(6 + j), half[:, par:par + 1], None, ALU.mult)\
                        .then_inc(S["kpad_v"], 1)
            v.wait_ge(S["gl_t"], 1)
            for seg, (branch, tile) in enumerate(((1, 1), (2, 1), (1, 0), (2, 0), (0, 0), (0, 1))):
                src = bank(0)[:, tile * 64 + branch * HEADS:tile * 64 + (branch + 1) * HEADS]
                v.tensor_scalar(gates[:, :, seg], src, 1.0, 0.5, ALU.add, ALU.mult).then_inc(S["gates_ready"], 1)
            for s in range(2):
                v.wait_ge(S["hid_tanh"], s + 1)
                v.scalar_tensor_tensor(hid[:, s, :], hidt[:, s, :], 1.0, bank(2 + s)[:, 0:2 * NC_BLOCKS], op0=ALU.add, op1=ALU.mult)\
                    .then_inc(S["hid_ready"], 1)
            v.wait_ge(S["kc_done"], 1)
            v.tensor_scalar(kcT[:, :, 0:NC_BLOCKS], bank(4)[:, 0:2 * NC_BLOCKS].rearrange("p (t n) -> p t n", t=2), 0.5, None, ALU.mult)\
                .then_inc(S["kc_ready"], 1)
            v.wait_ge(S["kc_done"], 2)
            v.tensor_scalar(vall[0:NC_BLOCKS, :, 4, :], bank(5)[0:NC_BLOCKS, 0:TOK].rearrange("p (g d) -> p g d", g=GROUPS), 0.5, None,
                            ALU.mult).then_inc(S["vall_ready"], 1)
            v.wait_ge(S["kcdup_done"], 1)
            for par in range(2):
                v.tensor_scalar(kcpad[:, par], bank(6)[:, 0:GROUPS * NCP].rearrange("p (g n) -> p g n", g=GROUPS),
                                half[:, par:par + 1], None, ALU.mult).then_inc(S["kcpad_ready"], 1)
            v.wait_ge(S["dist_ready"], 1)
            v.wait_ge(S["gates_ready"], 6)
            v.wait_ge(S["vall_ready"], 3)
            v.wait_ge(bank_free[1], 2)
            v.wait_ge(bank_free[0], 2)

            with v.Fori(0, GROUPS) as i:
                v.wait_ge(S["pv_done"], i * 4 + AHEAD)
                v.tensor_copy(qcur[:], qT[:, bass.ds(i * 2, 2), :])
                v.tensor_copy(slcur[:], slopes[:, bass.ds(i * REP, REP)])
                v.tensor_copy(gcur[:], gates[:, bass.ds(i * REP, REP), :])
                v.tensor_copy(vcur[:, :, HD:2 * HD], vall[:, bass.ds(i, 1), :, :].rearrange("p g s d -> p (g s) d"))\
                    .then_inc(S["qv_ready"], 1)
                v.wait_ge(S["qv_ready"], i + 1)
                thn = 0
                for j in range(8):
                    _, b, _, _, done, _ = panel("main", j, i)
                    if j in (0, 3):
                        thn += 1
                        v.wait_ge(S["th_ready"], i * 6 + thn)
                        v.scalar_tensor_tensor((za, None, None, zb)[j][:, bass.ds(i * 2, 2), :], th[:, b, :].rearrange("p (t n) -> p t n", t=2),
                                               1.0, tiles2(b), op0=ALU.add, op1=ALU.mult).then_inc(bank_free[b], 1)
                    elif j in (1, 2):
                        thn += 1
                        v.wait_ge(S["th_ready"], i * 6 + thn)
                        v.scalar_tensor_tensor(gin[:], th[:, b, :], 1.0 / GELU_C, bank(b), op0=ALU.add, op1=ALU.mult).then_inc(S["gin_ready"], 1)
                        thn += 1
                        v.wait_ge(S["th_ready"], i * 6 + thn)
                        v.scalar_tensor_tensor((uT, vT)[j - 1][:, bass.ds(i * 2, 2), :], th[:, b, :].rearrange("p (t n) -> p t n", t=2),
                                               1.0, tiles2(b), op0=ALU.add, op1=ALU.mult).then_inc(bank_free[b], 1)
                    if j < 4:
                        h, step = j, i * 24 + 6 * j
                        v.wait_ge(S["s_done"], i * 4 + (h + 1))
                        v.scalar_tensor_tensor(sT, dist[:], slcur[:, h:h + 1], pS[:, 0:800], op0=ALU.mult, op1=ALU.add).then_inc(S["s_free"], 1)
                        v.wait_ge(S["s_free"], i * 4 + (h + 2))
                        v.tensor_reduce(nmx[:, 0:2], sT[:, 0:512].rearrange("p (a n) -> p a n", a=2), AX.X, ALU.max, negate=True)
                        v.tensor_reduce(nmx[:, 2:4], sT[:, 512:768].rearrange("p (a n) -> p a n", a=2), AX.X, ALU.max, negate=True)
                        v.tensor_reduce(nmx[:, 4:6], sT[:, 768:800].rearrange("p (a n) -> p a n", a=2), AX.X, ALU.max, negate=True)\
                            .then_inc(S["t_ready"], 1)
                        v.wait_ge(S["exp_done"], i * 4 + (h + 1))
                        v.reciprocal(fac[:], sums[:]).then_inc(S["soft_step"], 1)
                        v.wait_ge(S["soft_step"], i * 12 + (3 * h + 1))
                        v.tensor_tensor(fac[:], fac[:], gcur[:, h, :], ALU.mult).then_inc(S["soft_step"], 1)
                        v.tensor_tensor(eT[:, 768:800], eT[:, 768:800], cmask[:], ALU.mult).then_inc(S["soft_step"], 1)
                        v.wait_ge(S["soft_step"], i * 12 + (3 * h + 3))
                        for at, size, f in ((0, TOK, 0), (512, P, 2), (768, NCP, 4)):
                            e = eT[:, at:at + 2 * size].rearrange("p (a n) -> p a n", a=2)
                            ins = v.tensor_tensor(e, e, fac[:, f:f + 2].unsqueeze(2).to_broadcast([P, 2, size]), ALU.mult)
                        ins.then_inc(S["e_ready"], 1)

            v.wait_ge(S["o_free"], 2 * GROUPS + 1)
            v.scalar_tensor_tensor(oaT, oaT, 0.5, za, op0=ALU.mult, op1=ALU.mult).then_inc(S["oa_ready"], 1)
            v.wait_ge(S["mean_done"], 1)
            v.scalar_tensor_tensor(vT, bank(2)[:, 0:TOK].unsqueeze(1).to_broadcast([P, BT, TOK]), -1.0 / B_WIDTH, vT,
                                   op0=ALU.mult, op1=ALU.add).then_inc(S["xc_ready"], 1)
            v.wait_ge(S["vrt_ready"], 1)
            do(v.reciprocal(rstd[:], rt[:]))
            do(v.tensor_tensor(vT, vT, rstd[:].unsqueeze(1).to_broadcast([P, BT, TOK]), ALU.mult))
            for n in range(BT):
                v.tensor_scalar(vT[:, n, :], vT[:, n, :], vec("ln_v_g", n), vec("ln_v_b", n), ALU.mult, ALU.add).then_inc(S["y_ready"], 1)
            for n in range(4):
                v.wait_ge(S["sv_done"], n + 1)
                do(v.scalar_tensor_tensor(uT[:, 2 * n:2 * n + 2, :], tiles2(4 + n), 0.25, uT[:, 2 * n:2 * n + 2, :],
                                          op0=ALU.mult, op1=ALU.mult))
            v.wait_ge(S["yt_done"], 4)
            v.tensor_tensor(obT, uT, zb, ALU.mult).then_inc(S["ob_ready"], 1)

            with v.Fori(0, 2) as i:
                for j in range(4):
                    _, b, _, _, done, _ = panel("up", j, i)
                    v.wait_ge(S["dense_done"], done)
                    t1, t2 = (th[:, n, :].rearrange("p (t n) -> p t n", t=2) for n in range(2))
                    v.scalar_tensor_tensor(t1, merge[:, bass.ds(i * 8 + 2 * j, 2), :], 1.0, tiles2(b), op0=ALU.add, op1=ALU.mult)
                    v.scalar_tensor_tensor(t2, merge[:, bass.ds(i * 8 + (KT + 2 * j), 2), :], 1.0, tiles2(2 + b), op0=ALU.add, op1=ALU.mult)\
                        .then_inc(bank_free[b], 1)
                    v.wait_ge(bank_free[b], i * 2 + (STARTS["up"][0] + j) // 2 + 1)
                    v.tensor_tensor(mergedT[:, bass.ds(i * 8 + 2 * j, 2), :], t1, t2, ALU.add).then_inc(S["up_done"], 1)
                    v.wait_ge(S["up_done"], i * 4 + (j + 1))
            v.wait_ge(S["xt2_ready"], 8)
            with v.Fori(0, 2) as i:
                for j in range(4):
                    _, b, _, _, done, _ = panel("out", j, i)
                    v.wait_ge(S["dense_done"], done)
                    x1 = x1T[:, bass.ds(i * 8 + 2 * j, 2), :]
                    v.scalar_tensor_tensor(x1, tiles2(b), 0.5, x1, op0=ALU.mult, op1=ALU.add).then_inc(bank_free[b], 1)
            with v.Fori(0, 2) as i:
                for j in range(4):
                    _, b, _, _, done, _ = panel("ple", j, i)
                    v.wait_ge(S["tg_looped"], i * 4 + (j + 1))
                    g1 = gin[:].rearrange("p (t n) -> p t n", t=2)
                    v.scalar_tensor_tensor(g1, th[:, b, :].rearrange("p (t n) -> p t n", t=2), 1.0, tiles2(2 + b), op0=ALU.add, op1=ALU.mult)\
                        .then_inc(bank_free[b], 1)
                    v.wait_ge(bank_free[b], i * 2 + (STARTS["ple"][0] + j) // 2 + 1)
                    v.scalar_tensor_tensor(x2T[:, bass.ds(i * 8 + 2 * j, 2), :], g1, 0.5, x1T[:, bass.ds(i * 8 + 2 * j, 2), :],
                                           op0=ALU.mult, op1=ALU.add).then_inc(S["x2_ready"], 1)
                    v.wait_ge(S["x2_ready"], i * 4 + (j + 1))
            norm(1, x2T, x2T, "final_g")
            norm(2, z2T, x2T, "norm1_g_2")

            lam = vec("lru_lambda_2")
            L = [lruC[:, 8 * n:8 * n + 8] for n in range(8)]
            do(v.tensor_scalar(L[0], lam, -1.0, None, ALU.mult))
            v.tensor_tensor(L[0], L[0], lam, ALU.max).then_inc(S["lam_abs"], 1)
            v.wait_ge(S["lam_u"], 1)
            do(v.tensor_scalar(L[2], L[1], 2.0, None, ALU.add))
            do(v.reciprocal(L[2], L[2]))
            do(v.tensor_tensor(L[1], L[1], L[2], ALU.mult))
            do(v.tensor_tensor(L[2], L[1], L[1], ALU.mult))
            do(v.tensor_scalar(L[3], L[2], 1.0 / 17, 1.0 / 15, ALU.mult, ALU.add))
            for m in (13, 11, 9, 7, 5, 3, 1):
                do(v.tensor_tensor(L[3], L[3], L[2], ALU.mult))
                do(v.tensor_scalar(L[3], L[3], 1.0 / m, None, ALU.add))
            do(v.tensor_tensor(L[3], L[3], L[1], ALU.mult))
            do(v.tensor_scalar(L[2], lam, 0.0, LRU_C / 2, ALU.min, ALU.mult))
            do(v.scalar_tensor_tensor(L[3], L[3], -LRU_C, L[2], op0=ALU.mult, op1=ALU.add))
            do(v.tensor_scalar(L[4], L[3], -1.0, None, ALU.mult))
            do(v.tensor_scalar(L[5], vec("gate_a_b_2"), 0.5, None, ALU.mult))
            v.tensor_scalar(L[6], vec("gate_x_b_2"), 0.5, None, ALU.mult).then_inc(S["lam_ready"], 1)
            start2 = STARTS["in2"][0]
            for b in range(2):
                v.wait_ge(bank_free[b], (start2 + 1 - b) // 2 + 2)
            for n in range(BT):
                do(v.tensor_scalar(xcT[:, n, :], xpad[:, n, 1:1 + TOK], vec("conv_w_2", n), vec("conv_b_2", n), ALU.mult, ALU.add))
            for k in range(1, CONV):
                for n in range(BT):
                    ins = v.scalar_tensor_tensor(xcT[:, n, :], xpad[:, n, 1 + k:1 + k + TOK], vec("conv_w_2", BT * k + n), xcT[:, n, :],
                                                 op0=ALU.mult, op1=ALU.add)
                    if k < CONV - 1:
                        ins.then_inc(S["uz_step"], 1)
                    else:
                        ins.then_inc(S["xc2_ready"], 1)
                if k < CONV - 1:
                    v.wait_ge(S["uz_step"], BT * k)
            for b in range(2):
                v.wait_ge(bank_free[b], (start2 + 1 - b) // 2 + 4)
            E_ = PAD + TOK
            do(v.tensor_tensor(sumA[:, :, 2:E_], upad[:, :, 2:E_], upad[:, :, 1:E_ - 1], ALU.add))
            do(v.tensor_tensor(sumB[:, :, 4:E_], sumA[:, 2:8, 4:E_], sumA[:, 2:8, 2:E_ - 2], ALU.add))
            do(v.tensor_tensor(sumA[:, 4:8, 8:E_], sumB[:, 2:6, 8:E_], sumB[:, 2:6, 4:E_ - 4], ALU.add))
            do(v.tensor_tensor(sumB[:, 4:6, PAD:E_], sumA[:, 6:8, PAD:E_], sumA[:, 6:8, 8:E_ - 8], ALU.add))
            for n, (w, src) in enumerate(zip(WINDOWS, (sumA[:, 0:2], sumB[:, 0:2], sumA[:, 4:6], sumB[:, 4:6]))):
                do(v.tensor_scalar(inv16[:, n, :], inv16[:, n, :], float(w), None, ALU.min))
                do(v.reciprocal(inv16[:, n, :], inv16[:, n, :]))
                tiles = slice(2 * n, 2 * n + 2)
                do(v.scalar_tensor_tensor(dT[:, tiles, :], src[:, :, PAD:E_], 1.0 / w, upad[:, tiles, PAD:E_], op0=ALU.mult, op1=ALU.subtract))
                head = dT[:, tiles, 0:PAD]
                do(v.tensor_tensor(head, src[:, :, PAD:2 * PAD], inv16[:, n, :].unsqueeze(1).to_broadcast([P, 2, PAD]), ALU.mult))
                do(v.tensor_tensor(head, head, upad[:, tiles, PAD:2 * PAD], ALU.subtract))
            v.sem_inc(S["pool_d"], 1)
            for j in range(4):
                _, b, _, _, done, _ = panel("in2", j, 2)
                v.wait_ge(S["th_ready"], 6 * GROUPS + 2 * j + 1)
                v.scalar_tensor_tensor(gin[:], th[:, b, :], 1.0 / GELU_C, bank(b), op0=ALU.add, op1=ALU.mult).then_inc(S["gin_ready"], 1)
                v.wait_ge(S["th_ready"], 6 * GROUPS + 2 * j + 2)
                v.scalar_tensor_tensor(gT[:, 2 * j:2 * j + 2, :], th[:, b, :].rearrange("p (t n) -> p t n", t=2), 1.0, tiles2(b),
                                       op0=ALU.add, op1=ALU.mult).then_inc(bank_free[b], 1)
            for n in range(4):
                v.wait_ge(S["pool_mm"], n + 1)
                for t in range(2):
                    v.tensor_scalar(yT[:, 2 * n + t, :], tiles2(6 + n % 2)[:, t, :], vec("pool_b_2", 2 * n + t), vec("pool_scale_2", 2 * n + t),
                                    ALU.add, ALU.mult).then_inc(S["pool_y"], 1)
            v.wait_ge(S["gate_evac"], 2 * BT)
            v.wait_ge(S["xc2_ready"], BT)
            do(v.scalar_tensor_tensor(tiT, tiT, 1.0, xcT, op0=ALU.add, op1=ALU.mult))
            v.wait_ge(S["rates_ready"], BT)
            do(v.tensor_tensor(trT, aT, aT, ALU.mult))
            v.scalar_tensor_tensor(multT, trT, 1.0, multT, op0=ALU.add, op1=ALU.mult).then_inc(S["mult2_ready"], 1)
            v.wait_ge(S["mult_ready"], 1)
            do(v.scalar_tensor_tensor(tiT, tiT, 0.5, multT, op0=ALU.mult, op1=ALU.mult))
            for n in range(BT):
                do(v.tensor_tensor_scan(xcT[:, n, :], aT[:, n, :], tiT[:, n, :], 0.0, ALU.mult, ALU.add))
            for b in range(2):
                v.wait_ge(bank_free[b], (start2 + 1 - b) // 2 + 6)
            v.scalar_tensor_tensor(yT[:, BT:KT, :], xcT, 0.5, gT, op0=ALU.mult, op1=ALU.mult).then_inc(S["lru_y"], 1)
            v.wait_ge(S["lru_y"], 1)
            with v.Fori(0, 2) as i:
                for j in range(4):
                    _, b, _, _, done, _ = panel("out2", j, i)
                    v.wait_ge(S["dense_done"], done)
                    cols = bass.ds(i * 8 + 2 * j, 2)
                    v.tensor_tensor(h2T[:, cols, :], tiles2(b), x2T[:, cols, :], ALU.add).then_inc(bank_free[b], 1)
                    v.wait_ge(bank_free[b], i * 2 + (STARTS["out2"][0] + j) // 2 + 1)
                    v.sem_inc(S["h2_ready"], 1)
            norm(3, z3T, h2T, "norm2_g_2")
            v.wait_ge(S["rtn_ready"], 1)
            do(v.reciprocal(rsn[:], rtn[:]))
            v.wait_ge(S["bc2_in"], 16)
            for hf in range(HALVES):
                v.scalar_tensor_tensor(znat[:, hf, :], hnat[:, hf, :], rsn[:, hf:hf + 1], g2bc, op0=ALU.mult, op1=ALU.mult)\
                    .then_inc(S["znat_ready"], 1)

            def choose(r, par, before):
                steps = [0]

                def step(ins):
                    steps[0] += 1
                    ins.then_inc(S["top_step"], 1)
                    v.wait_ge(S["top_step"], before + steps[0])
                    v.nop(nofuse=True)

                step(v.tensor_copy(row, scores[:, bass.ds(r, 1)].rearrange("p a s k -> p (a s) k")))

                def top16(values, spare, best, at):
                    step(v.max(best[:, 0:8], values))
                    step(v.max_index(at[:, 0:8], best[:, 0:8], values))
                    step(v.match_replace(spare, best[:, 0:8], values, LOWEST))
                    step(v.max(best[:, 8:16], spare))
                    step(v.max_index(at[:, 8:16], best[:, 8:16], spare))

                for s in range(2):
                    top16(row[:, s, :], row2[:, s, :], tv[:, s, :], ti_u[:, s, :])
                step(v.tensor_tensor(cand, tv[:, 0, :].unsqueeze(2).to_broadcast([P, TOPK, TOPK]),
                                     tv[:, 1, :].unsqueeze(1).to_broadcast([P, TOPK, TOPK]), ALU.add))
                flat, flat2 = (c.rearrange("p a b -> p (a b)") for c in (cand, cand2))
                top16(flat, flat2, top[:, par, :], pos[:])
                v.tensor_scalar(nm[:, par:par + 1], top[:, par, 0:1], -1.0, None, ALU.mult).then_inc(S["top_ready"], 1)
                step(v.tensor_copy(ti_f[:], ti_u[:]))
                step(v.tensor_scalar(posab[:, 0, :], pos[:], 4, None, ALU.logical_shift_right))
                step(v.tensor_scalar(posab[:, 1, :], pos[:], 15, None, ALU.bitwise_and))
                step(v.tensor_copy(posf[:], posab[:]))
                for s in range(2):
                    step(v.tensor_tensor(cand, posf[:, s, :].unsqueeze(2).to_broadcast([P, TOPK, TOPK]),
                                         iota16[:].unsqueeze(1).to_broadcast([P, TOPK, TOPK]), ALU.is_equal))
                    step(v.tensor_tensor(cand, cand, ti_f[:, s, :].unsqueeze(1).to_broadcast([P, TOPK, TOPK]), ALU.mult))
                    step(v.tensor_reduce(pick[:, s, :], cand, AX.X, ALU.add))
                step(v.scalar_tensor_tensor(expf[:], pick[:, 0, :], float(KEYS), pick[:, 1, :], op0=ALU.mult, op1=ALU.add))
                return steps[0]

            CHOOSE = 28
            v.wait_ge(S["sc_evac"], ROWS)
            v.wait_ge(S["sc_zero"], 1)
            v.wait_ge(S["znat_ready"], 2)
            for r in range(2):
                assert choose(r, r, CHOOSE * r) == CHOOSE
                v.tensor_copy(idx[:, r, :], expf[:]).then_inc(S["idx_ready"], 1)
            for hf in range(HALVES):
                with v.Fori(0, PEER_HEADS // 2) as i:
                    for par in range(2):
                        r = i * 2 + (PEER_HEADS * hf + par)
                        for k in range(TOPK):
                            s = k % 4
                            v.wait_ge(u_landed[s], r * 64 + 16 * (k // 4 + 1))
                            if k >= 2:
                                v.wait_ge(u_free[(k - 2) % 4], r * 4 + ((k - 2) // 4 + 2))
                            v.tensor_tensor_reduce(out=junk[k % 2], in0=ubuf[:, s, :], in1=znat[:, hf, :], scale=1.0, scalar=0.0,
                                                   op0=ALU.mult, op1=ALU.add, accum_out=act[:, par, k:k + 1]).then_inc(u_free[s], 1)
                        v.wait_ge(u_free[3], r * 4 + 5)
                        v.tensor_tensor(asq[:], act[:, par, :], act[:, par, :], ALU.mult).then_inc(S["gel_step"], 1)
                        v.wait_ge(S["gel_step"], r * 3 + 1)
                        v.scalar_tensor_tensor(ain[:, par, :], asq[:], 1.0 / GELU_C, act[:, par, :], op0=ALU.add, op1=ALU.mult)\
                            .then_inc(S["inner_ready"], 1)
                        v.wait_ge(S["ex_done"], r + 1)
                        v.reciprocal(er[:, par:par + 1], es[:, par:par + 1]).then_inc(S["gel_step"], 1)
                        v.wait_ge(S["gel_step"], r * 3 + 2)
                        v.scalar_tensor_tensor(agx[:, par, :], act[:, par, :], er[:, par:par + 1], eg[:, par, :], op0=ALU.mult, op1=ALU.mult)\
                            .then_inc(S["gel_step"], 1)
                        v.wait_ge(S["gel_step"], r * 3 + 3)
                        v.wait_ge(S["gel_done"], r + 1)
                        v.scalar_tensor_tensor(wk[:, par, :], ath[:, par, :], 1.0, agx[:, par, :], op0=ALU.add, op1=ALU.mult)\
                            .then_inc(S["w_ready"], 1)
                        choose(r + 2, par, r * CHOOSE + 2 * CHOOSE)
                        v.wait_ge(v_landed[3], r * 64 + 64)
                        v.tensor_copy(idx[:, par, :], expf[:]).then_inc(S["idx_ready"], 1)
                v.wait_ge(S["fin_rt"], hf + 1)
                do(v.reciprocal(rsn[:, hf:hf + 1], rtn[:, hf:hf + 1]))
                v.wait_ge(S["bcf_in"], 16)
                v.scalar_tensor_tensor(stage[:, hf, :], bank(4 * hf, 4), rsn[:, hf:hf + 1], gfbc, op0=ALU.mult, op1=ALU.mult)\
                    .then_inc(S["fin_out"], 1)

        @block.tensor
        def _(pe):
            mm, tr = nc.tensor.matmul, nc.tensor.transpose
            pe.sem_inc(S["s_free"], 1)
            pe.sem_inc(S["o_free"], 1)
            pe.sem_inc(S["pv_done"], AHEAD)

            def product(section, j, i, rhs, widths=(P, P), first=None):
                slot, b, landed, released, _, _ = panel(section, j, i)
                pe.wait_ge(w_landed[slot], landed)
                if STARTS[section][0] + j >= 2:
                    pe.wait_ge(bank_free[b], released)
                for t, w in enumerate(widths):
                    for k in range(KT):
                        if first is not None and t == 0:
                            pe.wait_ge(S["h_ready"], first + k + 1)
                        ins = mm(tiles2(b)[0:w, t, :], ring[:, slot, k, t * P:t * P + w], rhs[:, k, :], start=(k == 0), stop=(k == KT - 1))
                ins.then_inc(S["dense_done"], 1)

            def norm(n):
                pe.wait_ge(S["sq_ready"], n + 1)
                for k in range(KT):
                    ins = mm(bank(7)[:, 0:TOK], ones[:], sq[:, k, :], start=(k == 0), stop=(k == KT - 1))
                ins.then_inc(S["ss_done"], 1)

            pe.wait_ge(S["ident_ready"], 1)
            pe.wait_ge(S["vec_in"], 16 * (len(VEC_A) + len(VEC_B) + 2))
            tr(bank(0)[:, 0:P], vecA, ident[:])
            tr(bank(0)[:, P:VEC_COLS], vecB, ident[0:VEC_B_ROWS, 0:VEC_B_ROWS]).then_inc(S["vec_t"], 1)
            pe.wait_ge(S["x_in"], 16 * HALVES)
            for gi in range(KT):
                if gi >= 6:
                    pe.wait_ge(S["xt_evac_v" if gi % 2 else "xt_evac_a"], (gi - 6) // 2 + 1)
                for h in range(HALVES):
                    ins = tr(bank(2 + gi % 6)[:, h * P:(h + 1) * P], xnat0[:, h, gi * P:(gi + 1) * P], ident[:])
                ins.then_inc(S["xt_done"], 1)
            pe.wait_ge(S["ones_ready"], 3)
            norm(0)
            pe.wait_ge(S["vecs_ready"], 1)
            for j in range(4):
                product("q", j, 0, hT, first=0 if j == 0 else None)
            for j in range(6):
                product("kv", j, 0, hT)
            product("gl", 0, 0, hT, widths=(3 * HEADS,))
            for typ, which in enumerate((3, 5)):
                pe.wait_ge(S["kv_evac"], which + 1)
                for kt in range(2):
                    for t in range(2):
                        at = kt * TOK + t * P
                        ins = tr(bank(2 + typ)[:, at:at + P], kvT[:, which, t, kt * P:(kt + 1) * P], ident[:])
                ins.then_inc(S["vt_done"], 1)
            pe.wait_ge(S["dist_ready"], 1)
            for typ, which in enumerate((2, 4)):
                for t in range(2):
                    for s in range(2):
                        ins = mm(tiles2(4 + 2 * typ + t)[:, s, :], dup[:, s, :], kvT[:, which, t, :], start=True, stop=True)
                    ins.then_inc(S["dup_done"], 1)
            pe.wait_ge(S["gl_ready"], 1)
            for h in range(HALVES):
                ins = tr(bank(0)[:, h * 64:h * 64 + 3 * HEADS], glT[:, h * P:(h + 1) * P], ident[0:3 * HEADS, 0:3 * HEADS])
            ins.then_inc(S["gl_t"], 1)
            pe.wait_ge(S["cmp_in"], 16 * 8)
            pe.wait_ge(S["kab_ready"], 4)
            pe.wait_ge(S["vall_ready"], 2)
            for s in range(2):
                for l in range(CMP_LEN):
                    part, at = l // CMP_STRIDE, l % CMP_STRIDE
                    rhs = kab[:, 2 * s + part].rearrange("p t (n l) -> p t n l", l=CMP_STRIDE)[:, :, part:part + NC_BLOCKS, at]
                    ins = mm(bank(2 + s)[:, 0:2 * NC_BLOCKS], w1bd[:, s, l, :], rhs, start=(l == 0), stop=(l == CMP_LEN - 1))
                ins.then_inc(S["hid_done"], 1)
            pe.wait_ge(S["hid_ready"], 1)
            pe.wait_ge(S["kpad_a"], 4)
            mm(bank(4)[:, 0:2 * NC_BLOCKS], w2bd[:, 0, :], hid[:, 0, :], start=True, stop=True).then_inc(S["kc_done"], 1)
            pe.wait_ge(S["hid_ready"], 2)
            for t in range(2):
                ins = mm(bank(5)[0:NC_BLOCKS, t * P:(t + 1) * P], hid[:, 1, t * NC_BLOCKS:(t + 1) * NC_BLOCKS], w2bd[:, 1, :], start=True, stop=True)
            ins.then_inc(S["kc_done"], 1)
            pe.wait_ge(S["kc_ready"], 1)
            pe.wait_ge(S["kpad_v"], 4)
            for t in range(2):
                for s in range(2):
                    g = 2 * t + s
                    ins = mm(bank(6)[:, g * NCP:(g + 1) * NCP], dup[:, s, :], kcT[:, t, :], start=True, stop=True)
            ins.then_inc(S["kcdup_done"], 1)
            pe.wait_ge(S["kcpad_ready"], 2)
            pe.wait_ge(S["gates_ready"], 6)
            pe.wait_ge(S["vall_ready"], 3)

            with pe.Fori(0, GROUPS) as i:
                def head_scores(h):
                    pr, par = h // 2, h % 2
                    if h == 0:
                        pe.wait_ge(S["qv_ready"], i + 1)
                    pe.wait_ge(S["s_free"], i * 4 + (h + 1))
                    q0, q1 = qcur[:, pr, 0:P], qcur[:, pr, P:TOK]
                    mm(pS[:, 0:512], q1, kpad[:, par, :, bass.ds(i, 1), :].rearrange("p t g n -> p (t g) n"), start=True, stop=True)
                    mm(pS[:, 512:768], q0, kpad[:, par, :, bass.ds(i, 1), 0:P].rearrange("p t g n -> p (t g) n"), start=True, stop=True)
                    kc = kcpad[:, par, bass.ds(i, 1), :].rearrange("p g n -> p (g n)")
                    mm(pS[:, 768:784], q0, kc, start=True, stop=True)
                    mm(pS[:, 784:800], q1, kc, start=True, stop=True).then_inc(S["s_done"], 1)

                def head_turn(h):
                    pe.wait_ge(S["e_ready"], i * 4 + (h + 1))
                    for at, src in ((0, 512), (P, 0), (2 * P, 640), (3 * P, TOK), (4 * P, P), (5 * P, TOK + P)):
                        tr(pT_[:, at:at + P], eT[:, src:src + P], ident[:])
                    tr(pT_[0:NCP, 768:896], eT[:, 768:784], ident[:])
                    tr(pT_[0:NCP, 896:1024], eT[:, 784:800], ident[:]).then_inc(S["pt_done"], 1)

                def head_values(h):
                    par = h % 2
                    pe.wait_ge(S["pts_ready"], i * 4 + (h + 1))
                    if par == 0:
                        pe.wait_ge(S["o_free"], i * 2 + (h // 2 + 1))
                    cols = slice(0, P) if par else slice(HD, 3 * HD)
                    for n, (at, size, src) in enumerate(((0, TOK, 0), (P, P, 512), (0, TOK, TOK), (P, P, 640))):
                        mm(pO[:, at:at + size], vcur[:, n, cols], pts[:, src:src + size], start=(par == 0 and n == 0), stop=False,
                           skip_group_check=True)
                    mm(pO, vcur[0:NCP, 4, cols], pts[0:NCP, 768:1024], start=False, stop=(par == 1), skip_group_check=True)\
                        .then_inc(S["pv_done"], 1)

                for j in range(8):
                    product("main", j, i, hT)
                    if 2 <= j <= 5:
                        head_values(j - 2)
                    if 1 <= j <= 4:
                        head_turn(j - 1)
                    if j <= 3:
                        head_scores(j)

            start = STARTS["up"][0]
            for b in range(2):
                pe.wait_ge(bank_free[b], (start + 1 - b) // 2)
            for k in range(BT):
                ins = mm(bank(2)[:, 0:TOK], ones[:], vT[:, k, :], start=(k == 0), stop=(k == BT - 1))
            ins.then_inc(S["mean_done"], 1)
            pe.wait_ge(S["sgu_in"], 16)
            for n in range(2):
                for g in range(4):
                    ins = tr(bank(4 + n)[:, g * P:(g + 1) * P], sgun[:, 4 * n + g, :], ident[:])
                ins.then_inc(S["sgu_t"], 1)
            pe.wait_ge(S["vsq_ready"], 1)
            for k in range(BT):
                ins = mm(bank(3)[:, 0:TOK], ones[:], vsq[:, k, :], start=(k == 0), stop=(k == BT - 1))
            ins.then_inc(S["var_done"], 1)
            pe.wait_ge(S["sgu_t_evac"], 2)
            pe.wait_ge(S["y_ready"], BT)
            pe.wait_ge(S["o_free"], 2 * GROUPS + 1)
            for n in range(4):
                c, g0 = n // 2, 4 * (n % 2)
                for g in range(4):
                    ins = tr(bank(4 + n)[:, g * P:(g + 1) * P], vT[:, g0 + g, c * P:(c + 1) * P], ident[:])
                ins.then_inc(S["yt_done"], 1)
            pe.wait_ge(S["wt_ready"], 1)
            pe.wait_ge(S["sgub_in"], 16)
            pe.wait_ge(S["vn_ready"], 4)
            for n in range(4):
                for t in range(2):
                    g = 2 * n + t
                    for c in range(HALVES):
                        o = tiles2(4 + n)[:, t, c * P:(c + 1) * P]
                        mm(o, vn[:, c, g, :], sguT[:, g, :], start=True, stop=False)
                        ins = mm(o, ones[0:1, :], sgub[0:1, g * P:(g + 1) * P], start=False, stop=True)
                ins.then_inc(S["sv_done"], 1)

            pe.wait_ge(S["oa_ready"], 1)
            pe.wait_ge(S["ob_ready"], 1)
            with pe.Fori(0, 2) as i:
                for j in range(4):
                    slot, b, landed, released, _, _ = panel("up", j, i)
                    pe.wait_ge(w_landed[slot], landed)
                    pe.wait_ge(bank_free[b], released)
                    for t in range(2):
                        for src, at, o in ((oaT, 0, b), (obT, BT, 2 + b)):
                            for k in range(BT):
                                ins = mm(tiles2(o)[:, t, :], ring[:, slot, at + k, t * P:(t + 1) * P], src[:, k, :], start=(k == 0), stop=(k == BT - 1))
                    ins.then_inc(S["dense_done"], 1)
            pe.wait_ge(S["xnat_in"], 16 * HALVES)
            for n in range(8):
                if n >= 4:
                    pe.wait_ge(S["xt2_ready"], n - 3)
                for t in range(2):
                    for h in range(HALVES):
                        ins = tr(tiles2(4 + n % 4)[:, t, h * P:(h + 1) * P], xnat1[:, h, (2 * n + t) * P:(2 * n + t + 1) * P], ident[:])
                ins.then_inc(S["xt2_done"], 1)
            pe.wait_ge(S["up_done"], 8)
            with pe.Fori(0, 2) as i:
                for j in range(4):
                    product("out", j, i, mergedT)
            pe.wait_ge(S["pnat_in"], 16)
            pe.wait_ge(S["xt2_ready"], 8)
            for t in range(2):
                for h in range(HALVES):
                    ins = tr(tiles2(4)[:, t, h * P:(h + 1) * P], pnat[:, h, t * P:(t + 1) * P], ident[:])
            ins.then_inc(S["pt_t"], 1)
            pe.wait_ge(S["pt_ready"], 1)
            for b in range(2):
                pe.wait_ge(bank_free[b], (STARTS["ple"][0] + 1 - b) // 2)
            with pe.Fori(0, 2) as i:
                for j in range(4):
                    slot, b, landed, released, _, _ = panel("ple", j, i)
                    pe.wait_ge(w_landed[slot], landed)
                    pe.wait_ge(bank_free[b], released)
                    for t in range(2):
                        for k in range(2):
                            mm(tiles2(2 + b)[:, t, :], wple[:, slot, k, t * P:(t + 1) * P], pT[:, k, :], start=(k == 0), stop=(k == 1))
                        for k in range(KT):
                            ins = mm(tiles2(b)[:, t, :], ring[:, slot, k, t * P:(t + 1) * P], x1T[:, k, :], start=(k == 0), stop=(k == KT - 1))
                    ins.then_inc(S["dense_done"], 1)
            norm(1)
            norm(2)
            for j in range(4):
                product("in2", j, 0, z2T, first=2 * KT if j == 0 else None)
            with pe.Fori(1, 3) as i:
                for j in range(4):
                    product("in2", j, i, z2T)
            pe.wait_ge(S["blk2_in"], 48)
            for h in range(BT):
                pe.wait_ge(S["xc2_ready"], h + 1)
                if h >= 4:
                    pe.wait_ge(S["gate_evac"], 2 * (h - 3))
                mm(bank(2 + h % 4)[:, 0:TOK], gaw[:, h, :], xcT[:, h, :], start=True, stop=True)
                mm(bank(2 + h % 4)[:, TOK:2 * TOK], gxw[:, h, :], xcT[:, h, :], start=True, stop=True).then_inc(S["gate_mm"], 1)
            pe.wait_ge(S["pool_d"], 1)
            for n in range(4):
                if n >= 2:
                    pe.wait_ge(S["pool_y"], 2 * (n - 1))
                for t in range(2):
                    for k in range(2):
                        ins = mm(tiles2(6 + n % 2)[:, t, :], poolw[:, n, k, t * P:(t + 1) * P], dT[:, 2 * n + k, :], start=(k == 0), stop=(k == 1))
                ins.then_inc(S["pool_mm"], 1)
            pe.wait_ge(S["lru_y"], 1)
            pe.wait_ge(S["pool_y"], BT)
            with pe.Fori(0, 2) as i:
                for j in range(4):
                    product("out2", j, i, yT)
            pe.wait_ge(S["keys_in"], 32)
            pe.wait_ge(S["gate_evac"], 2 * BT)
            for n in range(4):
                for g in range(4):
                    ins = tr(bank(2 + n)[:, g * P:(g + 1) * P], keysn[:, n // 2, 4 * (n % 2) + g, :], ident[:])
                ins.then_inc(S["keys_t"], 1)
            norm(3)
            pe.wait_ge(S["keys_evac"], 4)
            for n in range(8):
                if n >= 4:
                    pe.wait_ge(S["hnat_ready"], n - 3)
                for t in range(4):
                    k = 4 * (n % 4) + t
                    ins = tr(bank(2 + n % 4)[:, t * P:(t + 1) * P], h2T[:, k, (n // 4) * P:(n // 4 + 1) * P], ident[:])
                ins.then_inc(S["h2t_done"], 1)
            pe.wait_ge(S["h_ready"], 4 * KT)
            with pe.Fori(0, 2) as i:
                for j in range(4):
                    product("wq", j, i, z3T)
            pe.wait_ge(S["qp_ready"], 8)
            pe.wait_ge(S["hnat_ready"], 8)
            for r in range(ROWS):
                hf, h = r // PEER_HEADS, r % PEER_HEADS
                if r >= 4:
                    pe.wait_ge(S["sc_evac"], r - 3)
                for s in range(2):
                    ins = mm(bank(2 + r % 4)[:, s * KEYS:(s + 1) * KEYS], qp[:, 2 * h + s, hf * P:(hf + 1) * P], keysT[:, s, h, :],
                             start=True, stop=True)
                ins.then_inc(S["sc_done"], 1)
            pe.wait_ge(S["sc_evac"], ROWS)
            for hf in range(HALVES):
                for c in range(4):
                    mm(bank(4 * hf + c), ident[:], hnat[:, hf, 512 * c:512 * (c + 1)], start=True, stop=False, skip_group_check=True)
                with pe.Fori(0, PEER_HEADS // 2) as i:
                    for par in range(2):
                        r = i * 2 + (PEER_HEADS * hf + par)
                        for k in range(TOPK):
                            s = k % 4
                            pe.wait_ge(diag_ready[s], r * 4 + (k // 4 + 1))
                            pe.wait_ge(v_landed[s], r * 64 + 16 * (k // 4 + 1))
                            for c in range(4):
                                ins = mm(bank(4 * hf + c), diag[:, s, :], vbuf[:, s, 512 * c:512 * (c + 1)], start=False, stop=True,
                                         skip_group_check=True)
                            ins.then_inc(v_free[s], 1)


_INS = ["x", "p", "norm_g", "w_in", "cmp_pe_k", "cmp_w1_k", "cmp_w2_k", "cmp_pe_v", "cmp_w1_v", "cmp_w2_v", "ln_v_g",
        "ln_v_b", "sgu_w", "sgu_b", "w_up_a", "w_up_b", "w_out", "w_ple", "w_ple_gate", "final_g", "norm1_g_2", "w_in_2",
        "pool_w_2", "pool_b_2", "pool_scale_2", "conv_w_2", "conv_b_2", "gate_a_w_2", "gate_a_b_2", "gate_x_w_2",
        "gate_x_b_2", "lru_lambda_2", "w_out_2", "norm2_g_2", "peer_wq_2", "peer_keys1_2", "peer_keys2_2", "peer_u_2",
        "peer_v_2", "norm_f_g_2"]


def kernel(**inputs):
    import concourse.bacc as bacc
    from concourse.bass_utils import run_bass_kernel_spmd

    nc = bacc.Bacc("TRN2", target_bir_lowering=False, num_devices=1)
    arrays, aps = {}, {}
    for name in _INS:
        a = np.ascontiguousarray(inputs[name])
        arrays[f"in_{name}"] = a
        aps[name] = nc.dram_tensor(f"in_{name}", a.shape, mybir.dt.from_np(a.dtype), kind="ExternalInput").ap()
    out = nc.dram_tensor("out", (1, TOK, D), mybir.dt.float32, kind="ExternalOutput").ap()
    build(nc, aps, out)
    result = run_bass_kernel_spmd(nc, [arrays], core_ids=[0])
    return result.results[0]["out"]
```

```python
from contextlib import ExitStack

import numpy as np

import concourse.bass as bass
from concourse import mybir

P = 128
TOK = 256
HALVES = TOK // P
D = 2048
KT = D // P
HEADS, GROUPS, HD = 16, 4, 64
REP = HEADS // GROUPS
A_WIDTH = HEADS * HD
B_WIDTH = D // 2
BT = B_WIDTH // P
CMP_LEN, CMP_STRIDE = 32, 16
NC_BLOCKS = TOK // CMP_STRIDE - CMP_LEN // CMP_STRIDE + 1
NCP = 16
PLE = 256
LRU_C = 8.0
CONV = 4
WINDOWS = (2, 4, 8, 16)
PAD = 16
PEER_HEADS, KEYS, TOPK = 8, 128, 16
EPS = 1e-6
MASKED = -1e30
LOWEST = -3.0e38
GELU_C = 0.044715
GELU_S = float(np.sqrt(2.0 / np.pi))

COL_Q = 0
COL_KV = COL_Q + A_WIDTH
COL_GL = COL_KV + 6 * GROUPS * HD
COL_ZA = COL_GL + 3 * HEADS
COL_U = COL_ZA + A_WIDTH
COL_V = COL_U + B_WIDTH
COL_ZB = COL_V + B_WIDTH
COL_MERGE = COL_ZB + B_WIDTH

PANEL = 2 * P
UNITS = 4
UNIT_KT = KT // 2
QUARTERS = 4
QUARTER_KT = KT // QUARTERS
SECTIONS = {
    "q": (4, 4), "gl": (1, 1), "kv": (6, 6), "main": (24, 6), "merge": (8, 8), "up": (8, 2),
    "out": (8, 2), "ple": (8, 2), "in2": (12, 12), "out2": (8, 2), "wq": (8, 8),
}


def section_starts():
    start, at = 0, {}
    for name, (panels, _) in SECTIONS.items():
        at[name] = start
        start += panels
    return at, start


STARTS, PANELS = section_starts()
STAGES = {name: n for n, name in enumerate(("h", "branches", "merged", "x1", "z2", "y", "z3"))}


def bank_of(section, j):
    return (STARTS[section] + j) % 2


def quarters_before(section, j, i=0):
    return i * (QUARTERS * SECTIONS[section][1]) + QUARTERS * (STARTS[section] + j)


def evacuated(section, j, i=0):
    return i * (SECTIONS[section][1] // 2) + (STARTS[section] + j) // 2


def unit_landed(section, j, i=0):
    return i * (8 * SECTIONS[section][1]) + 16 * ((STARTS[section] + j) // 2 + 1)


VEC_A = (("norm_g", 16), ("ln_v_g", 8), ("ln_v_b", 8), ("final_g", 16), ("norm1_g_2", 16), ("conv_w_2", 32),
         ("conv_b_2", 8), ("pool_b_2", 8), ("pool_scale_2", 8), ("gate_a_b_2", 8))
VEC_B = (("gate_x_b_2", 8), ("lru_lambda_2", 8), ("cmp_pe_k", 32), ("cmp_pe_v", 32), ("norm2_g_2", 16))


def vec_columns():
    at, col = {}, 0
    for name, rows in VEC_A + VEC_B:
        at[name] = (col, rows)
        col += rows
    return at, col


VEC_AT, VEC_COLS = vec_columns()
VEC_B_ROWS = VEC_COLS - P

ONCE = (
    "x_in", "vec_in", "sgu_in", "cmp_in", "pnat_in", "xnat_in", "wple_in", "blk2_in", "keys_in", "bc2_in", "bcf_in",
    "out_done",
    "ident_ready", "ones_ready", "dist_ready", "half_ready", "zero_ready", "w1_zeroed", "pad_zeroed", "wt_ready",
    "vec_t", "vecs_ready", "xss_ready", "xrt_ready", "xn_ready", "xt_done",
    "xh_ready", "x_ready", "sum_ready", "ss_done", "rt_ready",
    "kv_evac", "gl_ready", "gl_t", "gates_ready", "vt_done", "vall_ready", "dup_done", "kpad_a", "kpad_v",
    "kab_ready", "hid_done", "hid_tanh", "hid_ready", "kc_done", "kc_ready", "kcdup_done", "kcpad_ready",
    "mean_done", "xc_ready", "vsq_ready", "var_done", "vrt_ready", "y_ready", "yt_done", "vn_ready", "sv_done",
    "sgu_t", "sgu_t_evac", "ob_ready", "pt_t", "pt_ready", "xt2_done", "xt2_ready",
    "ss2_ready", "rs1_ready", "res_ready", "gx_ready", "pooled", "pool_mm", "pool_y", "xc2_ready", "lam_u", "lam_ready",
    "lam_abs", "inv_ready", "gate_mm", "gate_evac", "rates_ready", "mult2_ready", "mult_ready", "lru_y",
    "keys_t", "keys_evac", "h2t_done", "ssn_ready", "rtn_ready", "znat_ready", "sc_done",
    "sc_evac", "sc_zero", "fin_sq", "fin_rt", "fin_out",
)
LOOPED = (
    "wh_ready", "wl_ready", "w_used", "qv_ready", "th_ready", "gin_ready", "oa_ready", "s_done", "s_free", "t_ready", "exp_done", "e_ready",
    "pt_done", "pts_ready", "pv_done", "o_free", "up_done", "x1_ready", "tg_looped", "pg_done", "x2_ready", "h2_ready", "sq_step",
    "top_ready", "ex_done", "idx_ready", "inner_ready", "gel_done", "w_ready",
    "dve_step", "act_step", "pool_step", "uz_step", "soft_step", "top_step", "gel_step",
)
AHEAD = 4


def build(nc, T, out):
    f32, f32r, u32 = mybir.dt.float32, mybir.dt.float32r, mybir.dt.uint32
    ACT, ALU, AX = mybir.ActivationFunctionType, mybir.AluOpType, mybir.AxisListType
    ctx = ExitStack()
    with ctx:
        def sb(name, shape, dt=f32):
            return ctx.enter_context(nc.sbuf_tensor(name, shape, dt))

        S = {n: ctx.enter_context(nc.semaphore(n)) for n in ONCE + LOOPED}
        w_landed = [ctx.enter_context(nc.semaphore(f"w_landed{s}")) for s in range(UNITS)]
        bank_free = [ctx.enter_context(nc.semaphore(f"bank_free{b}")) for b in range(2)]
        u_landed = [ctx.enter_context(nc.semaphore(f"u_landed{s}")) for s in range(4)]
        u_free = [ctx.enter_context(nc.semaphore(f"u_free{s}")) for s in range(4)]
        v_landed = [ctx.enter_context(nc.semaphore(f"v_landed{s}")) for s in range(4)]
        v_free = [ctx.enter_context(nc.semaphore(f"v_free{s}")) for s in range(4)]
        diag_ready = [ctx.enter_context(nc.semaphore(f"diag_ready{s}")) for s in range(4)]

        with ExitStack() as dense:
            def split(name, *dims):
                return dense.enter_context(nc.sbuf_tensor(name, [P, *dims], f32r))

            WH, WL = split("WH", QUARTERS, QUARTER_KT, PANEL), split("WL", QUARTERS, QUARTER_KT, PANEL)
            XH, XL = split("XH", KT, TOK), split("XL", KT, TOK)
        EX = sb("EX", [P, 2 * QUARTERS * QUARTER_KT * PANEL + 2 * KT * TOK])
        RAW = sb("RAW", [P, UNITS * UNIT_KT * PANEL])
        RK = sb("RK", [P, 6144])
        RZ = sb("RZ", [P, 12352])
        RG = sb("RG", [P, 4096])

        def view(region, at, *dims):
            n = int(np.prod(dims))
            v = region[:, at:at + n]
            if len(dims) == 1:
                return v
            names = "abcd"[:len(dims)]
            return v.rearrange(f"p ({' '.join(names)}) -> p {' '.join(names)}", **dict(zip(names, dims)))

        raw = view(RAW, 0, UNITS, UNIT_KT, PANEL)
        xnat0 = view(RZ, 0, HALVES, D)
        xsq = [view(RG, 2048, D), view(RK, 0, D)]
        kvT = view(RZ, 0, 6, 2, TOK)
        w1bd = view(RZ, 3072, 2, CMP_LEN, P)
        kab = view(RG, 1280, 4, 2, TOK)
        qT = view(RK, 0, BT, TOK)
        oaT = qT
        kpad = view(RK, 2048, 2, 2, GROUPS, TOK)
        uT, vT = (view(RZ, 2048 * n, BT, TOK) for n in range(2))
        merge = view(RZ, 4096, 32, TOK)
        vall = view(RG, 0, GROUPS, 5, HD)
        sT = view(RG, 1280, 800)
        eT = view(RG, 2080, 800)
        pts = view(RG, 2880, 1024)
        sgub = RG[0:1, 1280:1280 + BT * P]
        sgun = view(RG, 2304, BT, P)
        sguT = sgun
        vsq = view(RK, 2048, BT, TOK)
        vn = view(RK, 4096, HALVES, BT, P)
        xnat1 = view(RK, 2048, HALVES, D)
        mergedT = view(RG, 0, KT, TOK)
        x1T = view(RZ, 0, KT, TOK)
        x2T = view(RZ, 4160, KT, TOK)
        wple = view(RZ, 8256, 2, D)
        pnat = view(RK, 0, HALVES, PLE)
        pT = view(RK, 512, 2, TOK)
        acc = view(RK, 2048, 2, 2, TOK)
        sqt = view(RK, 3072, 2, 2, TOK)
        xcT = view(RZ, 0, BT, TOK)
        xpad = view(RZ, 2048, BT, 4 + TOK)
        tiT = view(RZ, 2048, BT, TOK)
        upad = view(RZ, 8256, BT, PAD + TOK)
        sums2 = view(RZ, 10432, 2, 2, PAD + TOK)
        inv16 = view(RZ, 11584, 4, PAD)
        trT = view(RK, 2048, BT, TOK)
        multT = view(RK, 4096, BT, TOK)
        aT = view(RK, 0, BT, TOK)
        poolw = view(RG, 0, 4, 2, TOK)
        gaw = view(RG, 2048, BT, P)
        gxw = view(RG, 3072, BT, P)
        h2T = view(RZ, 0, KT, TOK)
        keysn = view(RK, 0, 2, PEER_HEADS, P)
        keysT = view(RG, 0, 2, PEER_HEADS, KEYS)
        g2bc = view(RG, 2048, D)
        qp = view(RZ, 8256, KT, TOK)
        znat = view(RZ, 4160, HALVES, D)
        ROWS = HALVES * PEER_HEADS
        scores = view(RK, 0, ROWS + 2, 2, KEYS)
        row = view(RK, 4608, 2, KEYS)
        row2 = view(RK, 4864, 2, KEYS)
        cand = view(RK, 5120, TOPK, TOPK)
        cand2 = view(RK, 5376, TOPK, TOPK)
        diag = view(RK, 5632, 4, P)
        junk = [view(EX, 0, D), view(EX, D, D)]
        gfbc = view(EX, 2 * D, D)
        ubuf = [view(RAW, (s + 2) % 4 * D, D) for s in range(4)]
        vbuf = [view(EX, (4 + s) * D, D) for s in range(4)]
        stage = view(RZ, 0, HALVES, D)

        ident = sb("ident", [P, P])
        identh = sb("identh", [P, P])
        vecA = view(RZ, 11264, P)
        vecB = RZ[0:VEC_B_ROWS, 11392:11392 + P]
        glT = RZ[0:3 * HEADS, 11520:11520 + TOK]
        w2bd = view(RZ, 11776, 2, P)
        dup = view(RZ, 12032, 2, P)
        ones = sb("ones", [P, P])
        half = sb("half", [P, 2])
        eps = sb("eps", [P, 2])
        dist = sb("dist", [P, 800])
        cmask = sb("cmask", [P, 32])
        slopes = sb("slopes", [P, HEADS])
        slcur = sb("slcur", [P, REP])
        gates = sb("gates", [P, HEADS, 6])
        lruC = gates[:].rearrange("p h s -> p (h s)")[:, 0:8 * BT]
        gcur = sb("gcur", [P, REP, 6])
        vecs = sb("vecs", [P, VEC_COLS])
        hid = sb("hid", [P, 2, 2 * NC_BLOCKS])
        hidt = sb("hidt", [P, 2, 2 * NC_BLOCKS])
        kcT = sb("kcT", [P, 2, NCP])
        kcpad = sb("kcpad", [P, 2, GROUPS, NCP])
        qcur = sb("qcur", [P, 2, TOK])
        vcur = sb("vcur", [P, 5, 3 * HD])
        th = sb("th", [P, 2, PANEL * 2])
        gin = sb("gin", [P, PANEL * 2])
        nmx = sb("nmx", [P, 6])
        sums = sb("sums", [P, 6])
        fac = sb("fac", [P, 6])
        rt = sb("rt", [P, TOK])
        rstd = sb("rstd", [P, TOK])
        g12 = sb("g12", [P, 2, KT])
        gT = [qcur[:], dist[:, 0:2 * TOK].rearrange("p (t n) -> p t n", t=2), view(RG, 3072, 2, TOK), view(RG, 3584, 2, TOK)]
        iota16 = sb("iota16", [P, TOPK])
        tv = sb("tv", [P, 2, TOPK])
        ti_u = sb("ti_u", [P, 2, TOPK], u32)
        ti_f = sb("ti_f", [P, 2, TOPK])
        top = sb("top", [P, 2, TOPK])
        pos = sb("pos", [P, TOPK], u32)
        posab = sb("posab", [P, 2, TOPK], u32)
        posf = sb("posf", [P, 2, TOPK])
        pick = sb("pick", [P, 2, TOPK])
        expf = sb("expf", [P, TOPK])
        idx = sb("idx", [P, 2, TOPK], u32)
        nm = sb("nm", [P, 2])
        eg = sb("eg", [P, 2, TOPK])
        es = sb("es", [P, 2])
        er = sb("er", [P, 2])
        act = sb("act", [P, 2, TOPK])
        asq = sb("asq", [P, TOPK])
        ain = sb("ain", [P, 2, TOPK])
        ath = sb("ath", [P, 2, TOPK])
        agx = sb("agx", [P, 2, TOPK])
        wk = sb("wk", [P, 2, TOPK])
        ssn = sb("ssn", [P, 2])
        rtn = sb("rtn", [P, 2])
        rsn = sb("rsn", [P, 2])

        PS = ctx.enter_context(nc.psum_tensor("PS", [P, 4096], f32))

        def bank(b, n=1):
            return PS[:, 512 * b:512 * (b + n)]

        def tiles2(b):
            return bank(b).rearrange("p (t n) -> p t n", t=2)

        pS = bank(2, 2)
        pT_ = bank(4, 2)
        pO = bank(6)[:, 0:TOK]

        def vec(name, n=None):
            c, rows = VEC_AT[name]
            return vecs[:, c:c + rows] if n is None else vecs[:, c + n:c + n + 1]

        def dview(a):
            return a.rearrange("(k p) n -> p k n", p=P)

        x_v = T["x"][0].rearrange("(h p) d -> p h d", p=P)
        w_in = dview(T["w_in"][0])
        w_in2 = dview(T["w_in_2"][0])
        up_a, up_b = dview(T["w_up_a"][0]), dview(T["w_up_b"][0])
        w_out, w_gate, w_ple = dview(T["w_out"][0]), dview(T["w_ple_gate"][0]), dview(T["w_ple"][0])
        w_out2, w_q = dview(T["w_out_2"][0]), dview(T["peer_wq_2"][0])
        peer_u, peer_v = T["peer_u_2"][0], T["peer_v_2"][0]

        def vec_rows(name):
            a = T[name]
            if name.startswith("cmp_pe"):
                return a[0]
            a = a if name == "final_g" else a[0]
            if len(a.shape) > 1:
                a = a.rearrange("a b -> (a b)")
            return a.rearrange("(k p) -> k p", p=P)

        block = ctx.enter_context(nc.Block())

        class Line:

            def __init__(self, eng, sem):
                self.eng, self.sem, self.n = eng, sem, 0

            def do(self, ins):
                self.n += 1
                ins.then_inc(self.sem, 1)
                self.eng.wait_ge(self.sem, self.n)

        def load_vectors(eng, buf, group):
            r = 0
            for name, rows in group:
                src = vec_rows(name)
                if name.startswith("cmp_pe"):
                    for s in range(2):
                        eng.dma_start(buf[r:r + rows, s * HD:(s + 1) * HD], src).then_inc(S["vec_in"], 16)
                else:
                    eng.dma_start(buf[r:r + rows, :], src).then_inc(S["vec_in"], 16)
                r += rows

        @block.sync
        def _(sp):
            def load(section, j, i, first, second):
                n = STARTS[section] + j
                for u, src in enumerate((first, second)):
                    slot = 2 * (n % 2) + u
                    if n >= 2:
                        sp.wait_ge(S["wl_ready"], quarters_before(section, j, i) + (2 * u + 2 - 2 * QUARTERS))
                    sp.dma_start(raw[:, slot], src).then_inc(w_landed[slot], 16)

            def load_rows(section, j, i, w, cols):
                load(section, j, i, w[:, 0:UNIT_KT, cols], w[:, UNIT_KT:KT, cols])

            for h in range(HALVES):
                sp.dma_start(xnat0[:, h, :], x_v[:, h, :]).then_inc(S["x_in"], 16)
            load_vectors(sp, vecB, VEC_B)
            for section, col in (("q", COL_Q), ("gl", COL_GL), ("kv", COL_KV)):
                for j in range(SECTIONS[section][0]):
                    load_rows(section, j, 0, w_in, slice(col + j * PANEL, col + (j + 1) * PANEL))
            with sp.Fori(0, GROUPS) as i:
                for j, (col, step) in enumerate(((COL_U, 1), (COL_ZB, 1), (COL_V, 1), (COL_MERGE, 2), (COL_MERGE + PANEL, 2), (COL_ZA, 1))):
                    load_rows("main", j, i, w_in, bass.ds(i * (step * PANEL) + col, PANEL))
            for j in range(8):
                if j == 2:
                    sp.wait_ge(S["o_free"], 2 * GROUPS + 1)
                    sp.dma_start(sgun, T["sgu_w"][0].rearrange("g t s -> t g s")).then_inc(S["sgu_in"], 16)
                    sp.dma_start(sgub, T["sgu_b"][0].rearrange("g t -> (g t)").unsqueeze(0)).then_inc(S["sgu_in"], 16)
                col = COL_MERGE + (8 + j) * PANEL
                load_rows("merge", j, 0, w_in, slice(col, col + PANEL))
            with sp.Fori(0, 4) as i:
                for j in range(2):
                    cols = bass.ds(i * (2 * PANEL) + j * PANEL, PANEL)
                    load("up", j, i, up_a[:, :, cols], up_b[:, :, cols])
            sp.wait_ge(S["sv_done"], 4)
            for h in range(HALVES):
                sp.dma_start(xnat1[:, h, :], x_v[:, h, :]).then_inc(S["xnat_in"], 16)
            sp.wait_ge(S["x_ready"], 4 * STAGES["branches"] + 2)
            sp.dma_start(pnat, T["p"][0][0].rearrange("(h p) d -> p h d", p=P)).then_inc(S["pnat_in"], 16)
            with sp.Fori(0, 4) as i:
                for j in range(2):
                    load_rows("out", j, i, w_out, bass.ds(i * (2 * PANEL) + j * PANEL, PANEL))
            sp.wait_ge(S["x_ready"], 4 * STAGES["merged"] + 4)
            sp.dma_start(wple, w_ple).then_inc(S["wple_in"], 16)
            sp.dma_start(poolw, T["pool_w_2"][0].rearrange("g (k p) n -> p g k n", p=P)).then_inc(S["blk2_in"], 16)
            sp.dma_start(gaw, T["gate_a_w_2"][0].rearrange("h p n -> p h n")).then_inc(S["blk2_in"], 16)
            sp.dma_start(gxw, T["gate_x_w_2"][0].rearrange("h p n -> p h n")).then_inc(S["blk2_in"], 16)
            with sp.Fori(0, 4) as i:
                for j in range(2):
                    load_rows("ple", j, i, w_gate, bass.ds(i * (2 * PANEL) + j * PANEL, PANEL))
            for n, col in enumerate((B_WIDTH, 0, 2 * B_WIDTH)):
                for j in range(4):
                    load_rows("in2", 4 * n + j, 0, w_in2, slice(col + j * PANEL, col + (j + 1) * PANEL))
            with sp.Fori(0, 4) as i:
                for j in range(2):
                    load_rows("out2", j, i, w_out2, bass.ds(i * (2 * PANEL) + j * PANEL, PANEL))
            sp.wait_ge(S["lru_y"], 4)
            sp.wait_ge(S["pool_y"], 4)
            for s, name in enumerate(("peer_keys1_2", "peer_keys2_2")):
                sp.dma_start(keysn[:, s], T[name][0].rearrange("h k d -> k h d")).then_inc(S["keys_in"], 16)
            sp.dma_start(g2bc, T["norm2_g_2"][0].partition_broadcast(P)).then_inc(S["bc2_in"], 16)
            for j in range(8):
                load_rows("wq", j, 0, w_q, slice(j * PANEL, (j + 1) * PANEL))
            sp.wait_ge(S["w_used"], QUARTERS * PANELS)
            sp.dma_start(gfbc, T["norm_f_g_2"].partition_broadcast(P)).then_inc(S["bcf_in"], 16)
            out_v = out[0].rearrange("(h p) d -> p h d", p=P)
            for h in range(HALVES):
                sp.wait_ge(S["fin_out"], h + 1)
                sp.dma_start(out_v[:, h, :], stage[:, h, :]).then_inc(S["out_done"], 16)
            sp.wait_ge(S["out_done"], 16 * HALVES)

        @block.gpsimd
        def _(g):
            line = Line(g, S["pool_step"])
            line.do(g.memset(ident[:], 0.0))
            g.affine_select(out=ident[:], in_=ident[:], compare_op=ALU.not_equal, fill=1.0, base=0,
                            pattern=[[-1, P]], channel_multiplier=1).then_inc(S["ident_ready"], 1)
            g.memset(ones[:], 1.0).then_inc(S["ones_ready"], 1)
            g.memset(eps[:, 0:1], EPS).then_inc(S["ones_ready"], 1)
            g.memset(eps[:, 1:2], 4 * EPS).then_inc(S["ones_ready"], 1)
            g.memset(half[:], 0.0).then_inc(S["zero_ready"], 1)
            g.memset(w2bd, 0.0).then_inc(S["zero_ready"], 1)
            g.memset(kcT[:], 0.0).then_inc(S["zero_ready"], 1)
            g.memset(vcur[:], 0.0).then_inc(S["zero_ready"], 1)
            g.memset(vall[:, :, 4, :], 0.0).then_inc(S["zero_ready"], 1)
            g.memset(dup, 0.0).then_inc(S["zero_ready"], 1)
            g.wait_ge(S["zero_ready"], 6)
            for s in range(2):
                v = dup[:, s, :].rearrange("p (a n) -> p a n", a=2)
                line.do(g.affine_select(out=v, in_=v, compare_op=ALU.not_equal, fill=1.0, base=-HD * s,
                                        pattern=[[0, 2], [-1, HD]], channel_multiplier=1))
            for s in range(2):
                line.do(g.memset(half[s * HD:(s + 1) * HD, s:s + 1], 1.0))
            g.sem_inc(S["half_ready"], 2)
            parts = ((0, 2, TOK, 1, -P), (512, 2, P, 1, 0), (768, 1, NCP, CMP_STRIDE, CMP_LEN - 1),
                     (784, 1, NCP, CMP_STRIDE, CMP_LEN - 1 - P))
            for at, reps, n, step, base in parts:
                v = dist[:, at:at + reps * n].rearrange("p (a n) -> p a n", a=reps)
                line.do(g.iota(v, pattern=[[0, reps], [step, n]], base=base, channel_multiplier=-1,
                               allow_small_or_imprecise_dtypes=True))
                line.do(g.affine_select(out=v, in_=v, compare_op=ALU.is_ge, fill=MASKED, base=-base,
                                        pattern=[[0, reps], [-step, n]], channel_multiplier=1))
            line.do(g.memset(cmask[:], 1.0))
            for s, base in enumerate((CMP_LEN - 1, CMP_LEN - 1 - P)):
                v = cmask[:, s * NCP:(s + 1) * NCP]
                line.do(g.affine_select(out=v, in_=v, compare_op=ALU.is_ge, fill=0.0, base=-base,
                                        pattern=[[-CMP_STRIDE, NCP]], channel_multiplier=1))
            for h in range(HEADS):
                line.do(g.memset(slopes[:, h:h + 1], float(np.float32(2.0) ** np.float32(-8.0 * (h + 1) / HEADS))))
            line.do(g.iota(iota16[:], pattern=[[1, TOPK]], base=0, channel_multiplier=0,
                           allow_small_or_imprecise_dtypes=True))
            line.do(g.memset(identh[:], 0.0))
            g.affine_select(out=identh[:], in_=identh[:], compare_op=ALU.not_equal, fill=0.5, base=0,
                            pattern=[[-1, P]], channel_multiplier=1).then_inc(S["dist_ready"], 1)
            g.wait_ge(S["xt_done"], 4)
            g.memset(w1bd, 0.0).then_inc(S["w1_zeroed"], 1)
            g.wait_ge(S["sgu_t_evac"], 2)
            g.affine_select(out=sguT, in_=sguT, compare_op=ALU.is_ge, fill=0.0, base=0,
                            pattern=[[0, BT], [1, P]], channel_multiplier=-1).then_inc(S["wt_ready"], 1)
            def squares(step, ready, src, i, j):
                g.wait_ge(S[ready], i * 4 + (j + 1))
                x = src[:, bass.ds(i * 8 + 2 * j, 2), :]
                step(g.tensor_tensor(sqt[:, 0], x, x, ALU.mult))
                step(g.tensor_tensor(acc[:, 0], acc[:, 0], sqt[:, 0], ALU.add))

            def stepper(before, i, per):
                count = [0]

                def step(ins):
                    count[0] += 1
                    ins.then_inc(S["sq_step"], 1)
                    g.wait_ge(S["sq_step"], i * per + (before + count[0]))
                return step

            g.wait_ge(S["vecs_ready"], 3)
            g.wait_ge(S["xt2_done"], 8)
            line.do(g.memset(acc, 0.0))
            with g.Fori(0, 2) as i:
                step = stepper(0, i, 16)
                for j in range(4):
                    squares(step, "x2_ready", x2T, i, j)
                    step(g.tensor_tensor(sqt[:, 1], sqt[:, 0], g12[:, 0, bass.ds(i * 8 + 2 * j, 2)].unsqueeze(2).to_broadcast([P, 2, TOK]), ALU.mult))
                    step(g.tensor_tensor(acc[:, 1], acc[:, 1], sqt[:, 1], ALU.add))
            g.sem_inc(S["sum_ready"], 1)
            g.wait_ge(S["x2_ready"], 8)
            for n in range(4):
                g.iota(inv16[:, n, :], pattern=[[1, PAD]], base=1, channel_multiplier=0,
                       allow_small_or_imprecise_dtypes=True).then_inc(S["pad_zeroed"], 1)
            g.memset(upad[:, :, 0:PAD], 0.0).then_inc(S["pad_zeroed"], 1)
            g.memset(xpad[:, :, 0:4], 0.0).then_inc(S["pad_zeroed"], 1)
            g.wait_ge(S["x_ready"], 4 * STAGES["z2"] + 4)
            g.wait_ge(S["rs1_ready"], 1)
            c1, _ = VEC_AT["final_g"]
            for c in range(4):
                x = x2T[:, 4 * c:4 * c + 4, :]
                line.do(g.tensor_tensor(x, x, vecs[:, c1 + 4 * c:c1 + 4 * c + 4].unsqueeze(2).to_broadcast([P, 4, TOK]), ALU.mult))
                g.tensor_tensor(x, x, th[:, 0, 0:TOK].unsqueeze(1).to_broadcast([P, 4, TOK]), ALU.mult).then_inc(S["res_ready"], 1)
            g.wait_ge(S["inv_ready"], 1)
            for n, w in enumerate(WINDOWS):
                if n:
                    g.wait_ge(S["pooled"], n)
                g.wait_ge(bank_free[bank_of("in2", 4 + n)], evacuated("in2", 4 + n) + 1)
                u = upad[:, 2 * n:2 * n + 2, :]
                src, reach = u, 1
                for step in range(n + 1):
                    dst = sums2[:, step % 2]
                    lo = 2 * reach
                    line.do(g.tensor_tensor(dst[:, :, lo:PAD + TOK], src[:, :, lo:PAD + TOK], src[:, :, lo - reach:PAD + TOK - reach], ALU.add))
                    src, reach = dst, lo
                d = sums2[:, (n + 1) % 2, :, 0:TOK]
                line.do(g.tensor_scalar(d[:, :, PAD:TOK], src[:, :, 2 * PAD:PAD + TOK], 1.0 / w, None, ALU.mult))
                line.do(g.tensor_tensor(d[:, :, 0:PAD], src[:, :, PAD:2 * PAD], inv16[:, n, :].unsqueeze(1).to_broadcast([P, 2, PAD]), ALU.mult))
                g.tensor_tensor(u[:, :, PAD:PAD + TOK], d, u[:, :, PAD:PAD + TOK], ALU.subtract).then_inc(S["pooled"], 1)
            g.wait_ge(S["lru_y"], 4)
            line.do(g.memset(acc, 0.0))
            with g.Fori(0, 2) as i:
                step = stepper(32, i, 8)
                for j in range(4):
                    squares(step, "h2_ready", h2T, i, j)
            g.sem_inc(S["sum_ready"], 1)
            g.memset(scores[:, ROWS:ROWS + 2], 0.0).then_inc(S["sc_zero"], 1)

            for s in range(4):
                g.sem_inc(u_free[s], 1)
                g.sem_inc(v_free[s], 1)

            def gather(table, buf, landed, free, r, par, k):
                s = k % 4
                g.wait_ge(free[s], r * 4 + (k // 4 + 1))
                g.nop(nofuse=True)
                g.indirect_dma_start(buf[s], None, table,
                                     bass.IndirectOffsetOnAxis(ap=idx[:, par, k:k + 1], axis=0)).then_inc(landed[s], 16)

            def gather_u(r, par, k):
                if k == 0:
                    g.wait_ge(S["idx_ready"], r + 1)
                gather(peer_u, ubuf, u_landed, u_free, r, par, k)

            LAG = 3

            def gather_row(r, par, last=False):
                for k in range(TOPK + LAG):
                    if k < TOPK:
                        gather(peer_v, vbuf, v_landed, v_free, r, par, k)
                    if k >= LAG and not last:
                        gather_u(r + 1, 1 - par, k - LAG)

            for k in range(TOPK):
                if k in (0, 2):
                    g.wait_ge(S["wl_ready"], QUARTERS * (PANELS - 1 + k // 2))
                gather_u(0, 0, k)
            g.wait_ge(S["w_used"], QUARTERS * PANELS)
            with g.Fori(0, ROWS // 2 - 1) as i:
                for par in range(2):
                    gather_row(i * 2 + par, par)
            gather_row(ROWS - 2, 0)
            gather_row(ROWS - 1, 1, last=True)

        @block.scalar
        def _(a):
            line = Line(a, S["act_step"])
            load_vectors(a, vecA, VEC_A)

            def split_next(section, j, i=0, ahead=1, quarters=range(QUARTERS)):
                n, before = STARTS[section] + j + ahead, quarters_before(section, j + ahead, i)
                for q in quarters:
                    slot = 2 * (n % 2) + q // 2
                    a.wait_ge(w_landed[slot], unit_landed(section, j + ahead, i))
                    if n >= 1:
                        a.wait_ge(S["w_used"], before + (q + 1 - QUARTERS))
                    at = QUARTER_KT * (q % 2)
                    a.activation(WH[:, q], raw[:, slot, at:at + QUARTER_KT, :], ACT.Copy).then_inc(S["wh_ready"], 1)

            def split_x(c, src, gain=None):
                x = src[:, 4 * c:4 * c + 4, :]
                if gain is None:
                    ins = a.activation(XH[:, 4 * c:4 * c + 4, :], x, ACT.Copy)
                else:
                    for k in range(4):
                        ins = a.activation(XH[:, 4 * c + k, :], x[:, k, :], ACT.Copy, scale=gain(4 * c + k))
                ins.then_inc(S["xh_ready"], 1)

            def last_panel(section, j, i, chunk, evac=None):
                split_next(section, j, i, quarters=range(3))
                done(section, j, i)
                chunk(0)
                if evac is not None:
                    evac()
                chunk(1)
                chunk(2)
                split_next(section, j, i, quarters=(3,))
                chunk(3)

            def done(section, j, i=0):
                a.wait_ge(S["w_used"], quarters_before(section, j + 1, i))

            a.wait_ge(S["x_in"], 16 * HALVES)
            a.activation(xsq[0], xnat0[:, 0, :], ACT.Square, accum_out=ssn[:, 0:1]).then_inc(S["xss_ready"], 1)
            a.wait_ge(S["xss_ready"], HALVES)
            a.wait_ge(S["ones_ready"], 3)
            a.activation(rtn[:], ssn[:], ACT.Sqrt, scale=1.0 / D, bias=eps[:, 0:1]).then_inc(S["xrt_ready"], 1)
            a.wait_ge(S["xrt_ready"], 2)
            a.activation(xnat0[:, 1, :], xnat0[:, 1, :], ACT.Copy, scale=rsn[:, 1:2]).then_inc(S["xn_ready"], 1)
            a.wait_ge(S["vecs_ready"], 1)
            for c in range(4):
                split_next("q", 0, 0, ahead=0, quarters=(c,))
                a.wait_ge(S["xt_done"], c + 1)
                for k in range(4):
                    ins = a.activation(XH[:, 4 * c + k, :], bank(2 + 2 * (c % 3), 2)[:, k * TOK:(k + 1) * TOK], ACT.Copy, scale=vec("norm_g", 4 * c + k))
                ins.then_inc(S["xh_ready"], 1)
            for j in range(4):
                split_next("q", j)
                b = bank_of("q", j)
                done("q", j)
                a.activation(qT[:, 2 * j:2 * j + 2, :], tiles2(b), ACT.Copy, scale=HD ** -0.5).then_inc(bank_free[b], 1)
            a.wait_ge(S["w1_zeroed"], 1)
            a.wait_ge(S["zero_ready"], 6)
            for s, kind in enumerate("kv"):
                for hf in range(2):
                    rows = slice(HD * hf, HD * (hf + 1))
                    a.dma_start(w1bd[rows, s, :, rows], T[f"cmp_w1_{kind}"][0].rearrange("l d e -> d l e")).then_inc(S["cmp_in"], 16)
                    a.dma_start(w2bd[rows, s, rows], T[f"cmp_w2_{kind}"][0]).then_inc(S["cmp_in"], 16)
            split_next("gl", 0)
            b = bank_of("gl", 0)
            done("gl", 0)
            line.do(a.activation(glT, bank(b)[0:3 * HEADS, 0:TOK], ACT.Tanh, scale=0.5))
            a.sem_inc(bank_free[b], 1)
            a.sem_inc(S["gl_ready"], 1)
            for j in range(6):
                split_next("kv", j)
                b = bank_of("kv", j)
                done("kv", j)
                line.do(a.activation(kvT[:, j, :, :], tiles2(b), ACT.Copy))
                a.sem_inc(bank_free[b], 1)
                a.sem_inc(S["kv_evac"], 1)
                if j == 3:
                    for s in range(2):
                        a.wait_ge(S["hid_done"], s + 1)
                        a.activation(hidt[:, s, :], bank(2 + s)[:, 0:2 * NC_BLOCKS], ACT.Tanh, scale=0.5).then_inc(S["hid_tanh"], 1)
            for j in range(2):
                a.wait_ge(S["dup_done"], j + 1)
                for par in range(2):
                    a.activation(kpad[:, par, 0, 2 * j:2 * j + 2, :], tiles2(4 + j), ACT.Copy,
                                 scale=half[:, par:par + 1]).then_inc(S["kpad_a"], 1)

            with a.Fori(0, GROUPS) as i:
                for j in range(6):
                    split_next("main", j, i)
                    b = bank_of("main", j)
                    done("main", j, i)
                    if j in (1, 5):
                        a.activation(th[:, b, :], bank(b), ACT.Tanh, scale=0.5).then_inc(S["th_ready"], 1)
                    elif j in (0, 2):
                        a.activation(th[:, b, :], bank(b), ACT.Square).then_inc(S["th_ready"], 1)
                        a.wait_ge(S["gin_ready"], i * 2 + (j // 2 + 1))
                        a.activation(th[:, b, :], gin[:], ACT.Tanh, scale=GELU_S * GELU_C).then_inc(S["th_ready"], 1)
                    else:
                        a.activation(merge[:, bass.ds(i * 4 + 2 * (j - 3), 2), :], tiles2(b), ACT.Tanh, scale=0.5)\
                            .then_inc(bank_free[b], 1)
                    if j in (3, 5):
                        a.wait_ge(S["pv_done"], i * 4 + (j - 1 + AHEAD))
                        a.activation(oaT[:, bass.ds(i * 2 + (j - 3) // 2, 1), :], pO.unsqueeze(1), ACT.Copy)\
                            .then_inc(S["o_free"], 1)
                    if 1 <= j <= 4:
                        h = j - 1
                        a.wait_ge(S["pt_done"], i * 4 + (h + 1))
                        a.wait_ge(S["pv_done"], i * 4 + (h + AHEAD))
                        a.activation(pts[:, 0:768], pT_[:, 0:768], ACT.Copy)
                        a.activation(pts[0:NCP, 768:1024], pT_[0:NCP, 768:1024], ACT.Copy).then_inc(S["pts_ready"], 1)
                    if j < 4:
                        a.wait_ge(S["t_ready"], i * 4 + (j + 1))
                        segments = ((0, TOK), (TOK, TOK), (512, P), (640, P), (768, NCP), (784, NCP))
                        for n, (at, size) in enumerate(segments):
                            ins = a.activation(eT[:, at:at + size], sT[:, at:at + size], ACT.Exp, bias=nmx[:, n:n + 1],
                                               accum_out=sums[:, n:n + 1])
                        ins.then_inc(S["exp_done"], 1)

            def merge_gate(j):
                a.activation(merge[:, 16 + 2 * j:18 + 2 * j, :], tiles2(bank_of("merge", j)), ACT.Tanh, scale=0.5)\
                    .then_inc(bank_free[bank_of("merge", j)], 1)

            for j in range(7):
                split_next("merge", j)
                done("merge", j)
                merge_gate(j)
                if j == 0:
                    a.wait_ge(S["xc_ready"], 1)
                    a.activation(vsq, vT, ACT.Square).then_inc(S["vsq_ready"], 1)
                if j == 1:
                    a.wait_ge(S["var_done"], 1)
                    a.activation(rt[:], bank(3)[:, 0:TOK], ACT.Sqrt, scale=1.0 / B_WIDTH, bias=eps[:, 1:2]).then_inc(S["vrt_ready"], 1)
                    for n in range(2):
                        a.wait_ge(S["sgu_t"], n + 1)
                        a.activation(sguT[:, 4 * n:4 * n + 4, :], bank(4 + n).rearrange("p (g n) -> p g n", g=4),
                                     ACT.Copy).then_inc(S["sgu_t_evac"], 1)
                if j == 3:
                    for n in range(4):
                        a.wait_ge(S["yt_done"], n + 1)
                        a.activation(vn[:, n // 2, 4 * (n % 2):4 * (n % 2) + 4, :], bank(4 + n).rearrange("p (g n) -> p g n", g=4),
                                     ACT.Copy).then_inc(S["vn_ready"], 1)
            def branches(c):
                a.wait_ge(*((S["oa_ready"], GROUPS) if c < 2 else (S["ob_ready"], 4)))
                x = oaT if c < 2 else uT
                a.activation(XH[:, 4 * c:4 * c + 4, :], x[:, 4 * (c % 2):4 * (c % 2) + 4, :], ACT.Copy).then_inc(S["xh_ready"], 1)

            last_panel("merge", 7, 0, branches, lambda: merge_gate(7))
            with a.Fori(0, 3) as i:
                for j in range(2):
                    split_next("up", j, i)
            split_next("up", 0, 3)

            def merged(c):
                a.wait_ge(S["up_done"], 2 * c + 2)
                split_x(c, mergedT)

            last_panel("up", 1, 3, merged)

            def turned_x(n):
                a.wait_ge(S["x_ready"], 4 * STAGES["branches"] + 4)
                a.wait_ge(S["xt2_done"], n + 1)
                a.activation(x1T[:, 2 * n:2 * n + 2, :], tiles2(4 + n % 4), ACT.Copy).then_inc(S["xt2_ready"], 1)

            for n in range(4):
                turned_x(n)
            split_next("out", 0, 0)
            for n in range(4, 8):
                turned_x(n)
            split_next("out", 1, 0)
            with a.Fori(1, 3) as i:
                for j in range(2):
                    split_next("out", j, i)
            split_next("out", 0, 3)
            a.wait_ge(S["lam_abs"], 1)
            a.activation(lruC[:, 8:16], lruC[:, 0:8], ACT.Exp, scale=-1.0).then_inc(S["lam_u"], 1)

            def x1(c):
                a.wait_ge(S["x1_ready"], 2 * c + 2)
                split_x(c, x1T)

            last_panel("out", 1, 3, x1)
            a.wait_ge(S["pt_t"], 1)
            a.activation(pT, tiles2(4), ACT.Copy).then_inc(S["pt_ready"], 1)

            def ple_gate(j, i):
                b = bank_of("ple", j)
                a.activation(th[:, b, :], bank(b), ACT.Tanh, scale=0.5).then_inc(S["tg_looped"], 1)

            with a.Fori(0, 3) as i:
                for j in range(2):
                    split_next("ple", j, i)
                    done("ple", j, i)
                    ple_gate(j, i)
            split_next("ple", 0, 3)
            done("ple", 0, 3)
            ple_gate(0, 3)

            def z2(c):
                a.wait_ge(S["x2_ready"], 2 * c + 2)
                split_x(c, x2T, lambda k: g12[:, 1, k:k + 1])

            last_panel("ple", 1, 3, z2, lambda: ple_gate(1, 3))
            def gates(heads):
                for h in heads:
                    a.wait_ge(S["gate_mm"], h + 1)
                    a.activation(trT[:, h, :], bank(2 + h % 4)[:, 0:TOK], ACT.Tanh, scale=0.5, bias=lruC[:, 40 + h:41 + h]).then_inc(S["gate_evac"], 1)
                    a.activation(tiT[:, h, :], bank(2 + h % 4)[:, TOK:2 * TOK], ACT.Tanh, scale=0.5, bias=lruC[:, 48 + h:49 + h])\
                        .then_inc(S["gate_evac"], 1)

            def rates(heads):
                for h in heads:
                    a.activation(aT[:, h, :], trT[:, h, :], ACT.Exp, scale=lruC[:, 24 + h:25 + h], bias=lruC[:, 24 + h:25 + h])
                    a.activation(multT[:, h, :], trT[:, h, :], ACT.Tanh, scale=lruC[:, 32 + h:33 + h], bias=lruC[:, 32 + h:33 + h])\
                        .then_inc(S["rates_ready"], 1)

            def next_y(c):
                y = upad[:, 4 * c:4 * c + 4, PAD:PAD + TOK] if c < 2 else xcT[:, 4 * c - BT:4 * c - BT + 4, :]
                a.activation(XH[:, 4 * c:4 * c + 4, :], y, ACT.Copy).then_inc(S["xh_ready"], 1)

            for j in range(12):
                if j in (7, 8):
                    step = gates if j == 7 else rates
                    step(range(0, 4))
                    split_next("in2", j, quarters=(0, 1))
                    step(range(4, 8))
                    split_next("in2", j, quarters=(2, 3))
                    if j == 7:
                        a.wait_ge(S["gate_evac"], 2 * BT)
                elif j < 11:
                    split_next("in2", j)
                else:
                    split_next("in2", j, quarters=range(3))
                    done("in2", j)
                    a.wait_ge(S["pool_y"], 4)
                    next_y(0)
                    next_y(1)
                    a.wait_ge(S["lru_y"], 2)
                    next_y(2)
                if j == 0:
                    a.wait_ge(S["ss_done"], 1)
                    a.activation(rt[:], bank(7)[:, 0:TOK], ACT.Sqrt, scale=1.0 / D, bias=eps[:, 0:1]).then_inc(S["rt_ready"], 1)
                    a.wait_ge(S["ss2_ready"], 1)
                    a.activation(rt[:], gin[:, 0:TOK], ACT.Sqrt, scale=1.0 / D, bias=eps[:, 0:1]).then_inc(S["rt_ready"], 1)
                if j == 6:
                    a.wait_ge(S["lam_ready"], 1)
                if j >= 8:
                    b = bank_of("in2", j)
                    if j == 8:
                        a.wait_ge(S["res_ready"], 4)
                    a.wait_ge(S["gx_ready"], j - 7)
                    t = th[:, b, :].rearrange("p (t n) -> p t n", t=2)
                    a.activation(t, gT[j - 8], ACT.Square).then_inc(S["th_ready"], 1)
                    a.wait_ge(S["gin_ready"], 2 * GROUPS + j - 7)
                    a.activation(th[:, b, :], gin[:], ACT.Tanh, scale=GELU_S * GELU_C).then_inc(S["th_ready"], 1)
                if j == 9:
                    a.wait_ge(S["mult2_ready"], 1)
                    a.activation(multT, multT, ACT.Sqrt).then_inc(S["mult_ready"], 1)
            split_next("in2", 11, quarters=(3,))
            a.wait_ge(S["lru_y"], 4)
            next_y(3)
            with a.Fori(0, 3) as i:
                for j in range(2):
                    split_next("out2", j, i)
            split_next("out2", 0, 3)

            def z3(c):
                a.wait_ge(S["h2_ready"], 2 * c + 2)
                split_x(c, h2T, lambda k: vec("norm2_g_2", k))

            last_panel("out2", 1, 3, z3)
            for n in range(4):
                a.wait_ge(S["keys_t"], n + 1)
                a.activation(keysT[:, n // 2, 4 * (n % 2):4 * (n % 2) + 4, :], bank(4 + n).rearrange("p (g n) -> p g n", g=4),
                             ACT.Copy).then_inc(S["keys_evac"], 1)

            def token_norm(hf):
                a.wait_ge(S["h2t_done"], hf + 1)
                a.activation(znat[:, hf, :], bank(2, 4), ACT.Square, accum_out=ssn[:, hf:hf + 1]).then_inc(S["ssn_ready"], 1)
                a.wait_ge(S["ssn_ready"], hf + 1)
                a.activation(rtn[:, hf:hf + 1], ssn[:, hf:hf + 1], ACT.Sqrt, scale=1.0 / D, bias=eps[:, 0:1]).then_inc(S["rtn_ready"], 1)

            def key_scores(h):
                a.wait_ge(S["sc_done"], h + 1)
                a.activation(scores[:, 0:ROWS].rearrange("p (f h) s k -> p f h (s k)", f=HALVES)[:, :, h, :], tiles2(6 + h % 2),
                             ACT.Copy).then_inc(S["sc_evac"], 1)

            for j in range(8):
                if j < 7:
                    split_next("wq", j)
                if j == 0:
                    a.wait_ge(S["ss_done"], 2)
                    a.activation(rt[:], bank(7)[:, 0:TOK], ACT.Sqrt, scale=1.0 / D, bias=eps[:, 0:1]).then_inc(S["rt_ready"], 1)
                    token_norm(0)
                if j == 2:
                    token_norm(1)
                if j:
                    key_scores(j - 1)
            key_scores(7)

            def expo(par, count):
                a.wait_ge(S["top_ready"], count)
                a.activation(eg[:, par, :], top[:, par, :], ACT.Exp, bias=nm[:, par:par + 1],
                             accum_out=es[:, par:par + 1]).then_inc(S["ex_done"], 1)

            expo(0, 1)
            expo(1, 2)
            for hf in range(HALVES):
                with a.Fori(0, PEER_HEADS // 2) as i:
                    for par in range(2):
                        r = i * 2 + (PEER_HEADS * hf + par)
                        a.wait_ge(S["inner_ready"], r + 1)
                        a.activation(ath[:, par, :], ain[:, par, :], ACT.Tanh, scale=GELU_S * GELU_C).then_inc(S["gel_done"], 1)
                        a.wait_ge(S["w_ready"], r + 1)
                        for k in range(TOPK):
                            s = k % 4
                            a.wait_ge(v_free[s], r * 4 + (k // 4 + 1))
                            a.activation(diag[:, s, :], identh[:], ACT.Copy, scale=wk[:, par, k:k + 1]).then_inc(diag_ready[s], 1)
                        expo(par, r + 3)
            for hf in range(HALVES):
                a.wait_ge(v_free[3], (hf + 1) * PEER_HEADS * 4 + 1)
                a.activation(stage[:, hf, :], bank(4 * hf, 4), ACT.Square, accum_out=ssn[:, hf:hf + 1]).then_inc(S["fin_sq"], 1)
                a.wait_ge(S["fin_sq"], hf + 1)
                a.activation(rtn[:, hf:hf + 1], ssn[:, hf:hf + 1], ACT.Sqrt, scale=1.0 / D, bias=eps[:, 0:1]).then_inc(S["fin_rt"], 1)

        @block.vector
        def _(v):
            line = Line(v, S["dve_step"])
            do = line.do

            def split_next(section, j, i=0, ahead=1, quarters=range(QUARTERS)):
                n, before = STARTS[section] + j + ahead, quarters_before(section, j + ahead, i)
                for q in quarters:
                    slot, at = 2 * (n % 2) + q // 2, QUARTER_KT * (q % 2)
                    v.wait_ge(S["wh_ready"], before + (q + 1))
                    v.tensor_tensor(WL[:, q], raw[:, slot, at:at + QUARTER_KT, :], WH[:, q].bitcast(f32), ALU.subtract).then_inc(S["wl_ready"], 1)

            def split_x(name, c, x, gain=None):
                v.wait_ge(S["xh_ready"], 4 * STAGES[name] + c + 1)
                if gain is None:
                    ins = v.tensor_tensor(XL[:, 4 * c:4 * c + 4, :], x, XH[:, 4 * c:4 * c + 4, :].bitcast(f32), ALU.subtract)
                else:
                    for k in range(4):
                        n = 4 * c + k
                        ins = v.scalar_tensor_tensor(XL[:, n, :], x[:, k, :], gain(n), XH[:, n, :].bitcast(f32), op0=ALU.mult, op1=ALU.subtract)
                ins.then_inc(S["x_ready"], 1)

            def last_panel(section, j, i, chunk, evac=None):
                split_next(section, j, i, quarters=range(3))
                chunk(0)
                if evac is not None:
                    evac()
                chunk(1)
                chunk(2)
                split_next(section, j, i, quarters=(3,))
                chunk(3)

            def done(section, j, i=0):
                v.wait_ge(S["w_used"], quarters_before(section, j + 1, i))

            v.wait_ge(S["x_in"], 16 * HALVES)
            v.tensor_tensor_reduce(out=xsq[1], in0=xnat0[:, 1, :], in1=xnat0[:, 1, :], scale=1.0, scalar=0.0, op0=ALU.mult, op1=ALU.add,
                                   accum_out=ssn[:, 1:2]).then_inc(S["xss_ready"], 1)
            v.wait_ge(S["xrt_ready"], 1)
            v.reciprocal(rsn[:], rtn[:]).then_inc(S["xrt_ready"], 1)
            v.wait_ge(S["xrt_ready"], 2)
            v.tensor_scalar(xnat0[:, 0, :], xnat0[:, 0, :], rsn[:, 0:1], None, ALU.mult).then_inc(S["xn_ready"], 1)
            v.wait_ge(S["vec_t"], 1)
            v.tensor_copy(vecs[:], bank(0)[:, 0:VEC_COLS]).then_inc(S["vecs_ready"], 1)
            v.wait_ge(S["vecs_ready"], 1)
            for c in range(4):
                split_next("q", 0, 0, ahead=0, quarters=(c,))
                split_x("h", c, bank(2 + 2 * (c % 3), 2).rearrange("p (k n) -> p k n", k=4), lambda k: vec("norm_g", k))
            v.tensor_tensor(g12[:, 0, :], vec("final_g"), vec("final_g"), ALU.mult).then_inc(S["vecs_ready"], 1)
            v.tensor_tensor(g12[:, 1, :], vec("final_g"), vec("norm1_g_2"), ALU.mult).then_inc(S["vecs_ready"], 1)
            for j in range(4):
                split_next("q", j)
            split_next("gl", 0)
            for j in range(6):
                split_next("kv", j)
                if j == 1:
                    v.wait_ge(S["gl_t"], 1)
                    for seg, (branch, tile) in enumerate(((1, 1), (2, 1), (1, 0), (2, 0), (0, 0), (0, 1))):
                        src = bank(7)[:, tile * 64 + branch * HEADS:tile * 64 + (branch + 1) * HEADS]
                        v.tensor_scalar(gates[:, :, seg], src, 1.0, 0.5, ALU.add, ALU.mult).then_inc(S["gates_ready"], 1)
                if j == 3:
                    for s in range(2):
                        v.wait_ge(S["hid_tanh"], s + 1)
                        v.scalar_tensor_tensor(hid[:, s, :], hidt[:, s, :], 1.0, bank(2 + s)[:, 0:2 * NC_BLOCKS], op0=ALU.add, op1=ALU.mult)\
                            .then_inc(S["hid_ready"], 1)
                if j == 4:
                    v.wait_ge(S["kc_done"], 1)
                    v.tensor_scalar(kcT[:, :, 0:NC_BLOCKS], bank(4)[:, 0:2 * NC_BLOCKS].rearrange("p (t n) -> p t n", t=2), 0.5, None, ALU.mult)\
                        .then_inc(S["kc_ready"], 1)
                    v.wait_ge(S["kc_done"], 2)
                    v.tensor_scalar(vall[0:NC_BLOCKS, :, 4, :], bank(5)[0:NC_BLOCKS, 0:TOK].rearrange("p (g d) -> p g d", g=GROUPS), 0.5, None,
                                    ALU.mult).then_inc(S["vall_ready"], 1)
                if j in (1, 2):
                    s, name = j - 1, ("cmp_pe_k", "cmp_pe_v")[j - 1]
                    v.wait_ge(S["kv_evac"], s + 1)
                    c, _ = VEC_AT[name]
                    for part in range(2):
                        pe = vecs[:, c + part * CMP_STRIDE:c + (part + 1) * CMP_STRIDE]
                        v.tensor_tensor(
                            kab[:, 2 * s + part].rearrange("p t (n l) -> p (t n) l", l=CMP_STRIDE),
                            kvT[:, s].rearrange("p t (n l) -> p (t n) l", l=CMP_STRIDE),
                            pe.unsqueeze(1).to_broadcast([P, 2 * TOK // CMP_STRIDE, CMP_STRIDE]), ALU.add).then_inc(S["kab_ready"], 1)
            def values(typ):
                v.wait_ge(S["vt_done"], typ + 1)
                v.tensor_copy(vall[:, :, 2 * typ:2 * typ + 2, :].rearrange("p g s d -> p s g d"),
                              bank(2 + typ).rearrange("p (s g d) -> p s g d", s=2, g=GROUPS)).then_inc(S["vall_ready"], 1)

            values(0)
            v.wait_ge(S["kcdup_done"], 1)
            for par in range(2):
                v.tensor_scalar(kcpad[:, par], bank(6)[:, 0:GROUPS * NCP].rearrange("p (g n) -> p g n", g=GROUPS),
                                half[:, par:par + 1], None, ALU.mult).then_inc(S["kcpad_ready"], 1)
            v.wait_ge(S["half_ready"], 2)
            for j in range(2):
                v.wait_ge(S["dup_done"], 3 + j)
                for par in range(2):
                    v.tensor_scalar(kpad[:, par, 1, 2 * j:2 * j + 2, :], tiles2(6 + j), half[:, par:par + 1], None, ALU.mult)\
                        .then_inc(S["kpad_v"], 1)
            values(1)
            v.wait_ge(S["dist_ready"], 1)
            v.wait_ge(S["gates_ready"], 6)
            v.wait_ge(S["vall_ready"], 3)
            v.wait_ge(S["kpad_a"], 4)
            v.wait_ge(bank_free[1], 2)
            v.wait_ge(bank_free[0], 2)

            with v.Fori(0, GROUPS) as i:
                v.wait_ge(S["pv_done"], i * 4 + AHEAD)
                v.tensor_copy(qcur[:], qT[:, bass.ds(i * 2, 2), :])
                v.tensor_copy(slcur[:], slopes[:, bass.ds(i * REP, REP)])
                v.tensor_copy(gcur[:], gates[:, bass.ds(i * REP, REP), :])
                v.tensor_copy(vcur[:, :, HD:2 * HD], vall[:, bass.ds(i, 1), :, :].rearrange("p g s d -> p (g s) d"))\
                    .then_inc(S["qv_ready"], 1)
                v.wait_ge(S["qv_ready"], i + 1)
                for j in range(6):
                    split_next("main", j, i)
                    b = bank_of("main", j)
                    t, g2 = th[:, b, :], gin[:].rearrange("p (t n) -> p t n", t=2)
                    pair = bass.ds(i * 2, 2)
                    if j in (0, 2):
                        first = 3 * (j // 2) + 1
                        v.wait_ge(S["th_ready"], i * 6 + first)
                        v.scalar_tensor_tensor(gin[:], t, 1.0 / GELU_C, bank(b), op0=ALU.add, op1=ALU.mult).then_inc(S["gin_ready"], 1)
                        v.wait_ge(S["th_ready"], i * 6 + (first + 1))
                        v.scalar_tensor_tensor((uT, vT)[j // 2][:, pair, :], t.rearrange("p (t n) -> p t n", t=2),
                                               1.0, tiles2(b), op0=ALU.add, op1=ALU.mult).then_inc(bank_free[b], 1)
                    elif j in (1, 5):
                        v.wait_ge(S["th_ready"], i * 6 + (3 if j == 1 else 6))
                        v.scalar_tensor_tensor(g2, t.rearrange("p (t n) -> p t n", t=2), 1.0, tiles2(b), op0=ALU.add, op1=ALU.mult)\
                            .then_inc(bank_free[b], 1)
                        v.wait_ge(bank_free[b], evacuated("main", j, i) + 1)
                        if j == 1:
                            v.wait_ge(bank_free[1 - b], evacuated("main", 0, i) + 1)
                            v.tensor_tensor(uT[:, pair, :], uT[:, pair, :], g2, ALU.mult).then_inc(S["uz_step"], 1)
                        else:
                            v.wait_ge(S["o_free"], i * 2 + 3)
                            v.scalar_tensor_tensor(oaT[:, pair, :], oaT[:, pair, :], 0.5, g2, op0=ALU.mult, op1=ALU.mult).then_inc(S["oa_ready"], 1)
                    if j < 4:
                        h = j
                        v.wait_ge(S["s_done"], i * 4 + (h + 1))
                        v.scalar_tensor_tensor(sT, dist[:], slcur[:, h:h + 1], pS[:, 0:800], op0=ALU.mult, op1=ALU.add).then_inc(S["s_free"], 1)
                        v.wait_ge(S["s_free"], i * 4 + (h + 2))
                        v.tensor_reduce(nmx[:, 0:2], sT[:, 0:512].rearrange("p (a n) -> p a n", a=2), AX.X, ALU.max, negate=True)
                        v.tensor_reduce(nmx[:, 2:4], sT[:, 512:768].rearrange("p (a n) -> p a n", a=2), AX.X, ALU.max, negate=True)
                        v.tensor_reduce(nmx[:, 4:6], sT[:, 768:800].rearrange("p (a n) -> p a n", a=2), AX.X, ALU.max, negate=True)\
                            .then_inc(S["t_ready"], 1)
                        v.wait_ge(S["exp_done"], i * 4 + (h + 1))
                        v.reciprocal(fac[:], sums[:]).then_inc(S["soft_step"], 1)
                        v.wait_ge(S["soft_step"], i * 12 + (3 * h + 1))
                        v.tensor_tensor(fac[:], fac[:], gcur[:, h, :], ALU.mult).then_inc(S["soft_step"], 1)
                        v.tensor_tensor(eT[:, 768:800], eT[:, 768:800], cmask[:], ALU.mult).then_inc(S["soft_step"], 1)
                        v.wait_ge(S["soft_step"], i * 12 + (3 * h + 3))
                        for at, size, f in ((0, TOK, 0), (512, P, 2), (768, NCP, 4)):
                            e = eT[:, at:at + 2 * size].rearrange("p (a n) -> p a n", a=2)
                            ins = v.tensor_tensor(e, e, fac[:, f:f + 2].unsqueeze(2).to_broadcast([P, 2, size]), ALU.mult)
                        ins.then_inc(S["e_ready"], 1)

            v.wait_ge(S["mean_done"], 1)
            v.scalar_tensor_tensor(vT, bank(2)[:, 0:TOK].unsqueeze(1).to_broadcast([P, BT, TOK]), -1.0 / B_WIDTH, vT,
                                   op0=ALU.mult, op1=ALU.add).then_inc(S["xc_ready"], 1)
            for j in range(7):
                split_next("merge", j)
                if j == 1:
                    v.wait_ge(S["vrt_ready"], 1)
                    do(v.reciprocal(rstd[:], rt[:]))
                    do(v.tensor_tensor(vT, vT, rstd[:].unsqueeze(1).to_broadcast([P, BT, TOK]), ALU.mult))
                    for n in range(BT):
                        v.tensor_scalar(vT[:, n, :], vT[:, n, :], vec("ln_v_g", n), vec("ln_v_b", n), ALU.mult, ALU.add).then_inc(S["y_ready"], 1)
                if j == 5:
                    v.wait_ge(S["uz_step"], GROUPS)
                    for n in range(4):
                        v.wait_ge(S["sv_done"], n + 1)
                        v.scalar_tensor_tensor(uT[:, 2 * n:2 * n + 2, :], tiles2(4 + n), 0.25, uT[:, 2 * n:2 * n + 2, :],
                                               op0=ALU.mult, op1=ALU.mult).then_inc(S["ob_ready"], 1)

            def branches(c):
                x = oaT if c < 2 else uT
                split_x("branches", c, x[:, 4 * (c % 2):4 * (c % 2) + 4, :])

            last_panel("merge", 7, 0, branches)

            def merged(j, i):
                b = bank_of("up", j)
                done("up", j, i)
                t1, t2 = (th[:, n, :].rearrange("p (t n) -> p t n", t=2) for n in range(2))
                v.scalar_tensor_tensor(t1, merge[:, bass.ds(i * 4 + 2 * j, 2), :], 1.0, tiles2(b), op0=ALU.add, op1=ALU.mult)
                v.scalar_tensor_tensor(t2, merge[:, bass.ds(i * 4 + (KT + 2 * j), 2), :], 1.0, tiles2(2 + b), op0=ALU.add, op1=ALU.mult)\
                    .then_inc(bank_free[b], 1)
                v.wait_ge(bank_free[b], evacuated("up", j, i) + 1)
                v.tensor_tensor(mergedT[:, bass.ds(i * 4 + 2 * j, 2), :], t1, t2, ALU.add).then_inc(S["up_done"], 1)
                v.wait_ge(S["up_done"], i * 2 + (j + 1))

            with v.Fori(0, 3) as i:
                for j in range(2):
                    split_next("up", j, i)
                    merged(j, i)
            split_next("up", 0, 3)
            merged(0, 3)
            last_panel("up", 1, 3, lambda c: split_x("merged", c, mergedT[:, 4 * c:4 * c + 4, :]), lambda: merged(1, 3))

            def x1(j, i):
                b = bank_of("out", j)
                done("out", j, i)
                v.wait_ge(S["xt2_ready"], 8)
                x = x1T[:, bass.ds(i * 4 + 2 * j, 2), :]
                v.scalar_tensor_tensor(x, tiles2(b), 0.5, x, op0=ALU.mult, op1=ALU.add).then_inc(bank_free[b], 1)
                v.wait_ge(bank_free[b], evacuated("out", j, i) + 1)
                v.sem_inc(S["x1_ready"], 1)

            with v.Fori(0, 3) as i:
                for j in range(2):
                    split_next("out", j, i)
                    x1(j, i)
            split_next("out", 0, 3)
            x1(0, 3)
            lam = vec("lru_lambda_2")
            L = [lruC[:, 8 * n:8 * n + 8] for n in range(8)]
            do(v.tensor_scalar(L[0], lam, -1.0, None, ALU.mult))
            v.tensor_tensor(L[0], L[0], lam, ALU.max).then_inc(S["lam_abs"], 1)
            v.wait_ge(S["lam_u"], 1)
            do(v.tensor_scalar(L[2], L[1], 2.0, None, ALU.add))
            do(v.reciprocal(L[2], L[2]))
            do(v.tensor_tensor(L[1], L[1], L[2], ALU.mult))
            do(v.tensor_tensor(L[2], L[1], L[1], ALU.mult))
            do(v.tensor_scalar(L[3], L[2], 1.0 / 17, 1.0 / 15, ALU.mult, ALU.add))
            for m in (13, 11, 9, 7, 5, 3, 1):
                do(v.tensor_tensor(L[3], L[3], L[2], ALU.mult))
                do(v.tensor_scalar(L[3], L[3], 1.0 / m, None, ALU.add))
            do(v.tensor_tensor(L[3], L[3], L[1], ALU.mult))
            do(v.tensor_scalar(L[2], lam, 0.0, LRU_C / 2, ALU.min, ALU.mult))
            do(v.scalar_tensor_tensor(L[3], L[3], -LRU_C, L[2], op0=ALU.mult, op1=ALU.add))
            do(v.tensor_scalar(L[4], L[3], -1.0, None, ALU.mult))
            do(v.tensor_scalar(L[5], vec("gate_a_b_2"), 0.5, None, ALU.mult))
            v.tensor_scalar(L[6], vec("gate_x_b_2"), 0.5, None, ALU.mult).then_inc(S["lam_ready"], 1)
            last_panel("out", 1, 3, lambda c: split_x("x1", c, x1T[:, 4 * c:4 * c + 4, :]), lambda: x1(1, 3))

            def x2(j, i):
                b = bank_of("ple", j)
                v.wait_ge(S["tg_looped"], i * 2 + (j + 1))
                v.wait_ge(S["pg_done"], i * 2 + (j + 1))
                g1 = gin[:].rearrange("p (t n) -> p t n", t=2)
                v.scalar_tensor_tensor(g1, th[:, b, :].rearrange("p (t n) -> p t n", t=2), 1.0, tiles2(2 + b), op0=ALU.add, op1=ALU.mult)\
                    .then_inc(bank_free[b], 1)
                v.wait_ge(bank_free[b], evacuated("ple", j, i) + 1)
                cols = bass.ds(i * 4 + 2 * j, 2)
                v.scalar_tensor_tensor(x2T[:, cols, :], g1, 0.5, x1T[:, cols, :], op0=ALU.mult, op1=ALU.add).then_inc(S["x2_ready"], 1)
                v.wait_ge(S["x2_ready"], i * 2 + (j + 1))

            with v.Fori(0, 3) as i:
                for j in range(2):
                    split_next("ple", j, i)
                    x2(j, i)
            split_next("ple", 0, 3)
            x2(0, 3)
            last_panel("ple", 1, 3, lambda c: split_x("z2", c, x2T[:, 4 * c:4 * c + 4, :], lambda k: g12[:, 1, k:k + 1]), lambda: x2(1, 3))
            split_next("in2", 0)
            v.wait_ge(S["rt_ready"], 1)
            do(v.reciprocal(rstd[:], rt[:]))
            g_a, g_b = gin[:, 0:TOK], gin[:, TOK:2 * TOK]
            do(v.tensor_tensor(g_b, rstd[:], rstd[:], ALU.mult))
            v.tensor_tensor(g_a, bank(7)[:, TOK:2 * TOK], g_b, ALU.mult).then_inc(S["ss2_ready"], 1)
            v.tensor_copy(th[:, 0, 0:TOK], rstd[:]).then_inc(S["rs1_ready"], 1)
            v.wait_ge(S["rs1_ready"], 1)
            v.wait_ge(S["rt_ready"], 2)
            do(v.reciprocal(rstd[:], rt[:]))
            do(v.tensor_tensor(rstd[:], rstd[:], th[:, 0, 0:TOK], ALU.mult))
            rstd2 = rstd[:].unsqueeze(1).to_broadcast([P, 2, TOK])
            v.wait_ge(S["pad_zeroed"], 6)

            def in2(j):
                b = bank_of("in2", j)
                done("in2", j)
                n = 2 * (j % 4)
                dst = (xpad[:, n:n + 2, 4:4 + TOK], upad[:, n:n + 2, PAD:PAD + TOK], gT[j % 4])[j // 4]
                v.tensor_tensor(dst, tiles2(b), rstd2, ALU.mult).then_inc(bank_free[b], 1)

            in2(0)
            split_next("in2", 1)
            in2(1)
            for n, w in enumerate(WINDOWS):
                do(v.tensor_scalar(inv16[:, n, :], inv16[:, n, :], float(w), None, ALU.min))
            v.reciprocal(inv16[:], inv16[:]).then_inc(S["inv_ready"], 1)
            split_next("in2", 2)
            in2(2)
            split_next("in2", 3)
            in2(3)
            for j in (4, 5):
                v.wait_ge(bank_free[bank_of("in2", j)], evacuated("in2", j))
            for n in range(BT):
                do(v.tensor_scalar(xcT[:, n, :], xpad[:, n, 1:1 + TOK], vec("conv_w_2", n), vec("conv_b_2", n), ALU.mult, ALU.add))
            for k in range(1, CONV):
                for n in range(BT):
                    ins = v.scalar_tensor_tensor(xcT[:, n, :], xpad[:, n, 1 + k:1 + k + TOK], vec("conv_w_2", BT * k + n), xcT[:, n, :],
                                                 op0=ALU.mult, op1=ALU.add)
                    if k < CONV - 1:
                        ins.then_inc(S["uz_step"], 1)
                    else:
                        ins.then_inc(S["xc2_ready"], 1)
                if k < CONV - 1:
                    v.wait_ge(S["uz_step"], GROUPS + BT * k)
                if k < 3:
                    split_next("in2", 3 + k)
                    in2(3 + k)
            split_next("in2", 6)
            in2(6)
            split_next("in2", 7)
            in2(7)
            v.wait_ge(S["gate_evac"], 2 * BT)
            v.wait_ge(S["xc2_ready"], BT)
            do(v.scalar_tensor_tensor(tiT, tiT, 1.0, xcT, op0=ALU.add, op1=ALU.mult))

            def gate(j):
                b, g = bank_of("in2", j), gT[j - 8]
                in2(j)
                v.wait_ge(bank_free[b], evacuated("in2", j) + 1)
                v.sem_inc(S["gx_ready"], 1)
                t, g2 = (x.rearrange("p (t n) -> p t n", t=2) for x in (th[:, b, :], gin[:]))
                v.wait_ge(S["th_ready"], 6 * GROUPS + 2 * (j - 8) + 1)
                v.scalar_tensor_tensor(g2, t, 1.0 / GELU_C, g, op0=ALU.add, op1=ALU.mult).then_inc(S["gin_ready"], 1)
                v.wait_ge(S["th_ready"], 6 * GROUPS + 2 * (j - 8) + 2)
                v.scalar_tensor_tensor(g, t, 1.0, g, op0=ALU.add, op1=ALU.mult).then_inc(S["uz_step"], 1)

            split_next("in2", 8)
            gate(8)
            split_next("in2", 9)
            v.wait_ge(S["rates_ready"], BT)
            do(v.tensor_tensor(trT, aT, aT, ALU.mult))
            v.scalar_tensor_tensor(multT, trT, 1.0, multT, op0=ALU.add, op1=ALU.mult).then_inc(S["mult2_ready"], 1)
            gate(9)
            for n in range(4):
                v.wait_ge(S["pool_mm"], n + 1)
                for t in range(2):
                    ins = v.tensor_scalar(upad[:, 2 * n + t, PAD:PAD + TOK], tiles2(2 + n)[:, t, :], vec("pool_b_2", 2 * n + t),
                                          vec("pool_scale_2", 2 * n + t), ALU.add, ALU.mult)
                ins.then_inc(S["pool_y"], 1)
            split_next("in2", 10)
            gate(10)
            v.wait_ge(S["mult_ready"], 1)
            do(v.scalar_tensor_tensor(tiT, tiT, 0.5, multT, op0=ALU.mult, op1=ALU.mult))
            split_next("in2", 11, quarters=(0,))
            for n in range(BT):
                do(v.tensor_tensor_scan(xcT[:, n, :], aT[:, n, :], tiT[:, n, :], 0.0, ALU.mult, ALU.add))

            def gated(n):
                pair = slice(2 * n, 2 * n + 2)
                v.wait_ge(S["uz_step"], GROUPS + 2 * BT + n + 1)
                v.scalar_tensor_tensor(xcT[:, pair, :], xcT[:, pair, :], 0.5, gT[n], op0=ALU.mult, op1=ALU.mult).then_inc(S["lru_y"], 1)

            split_x("y", 0, upad[:, 0:4, PAD:PAD + TOK])
            split_next("in2", 11, quarters=(1,))
            split_x("y", 1, upad[:, 4:8, PAD:PAD + TOK])
            for n in range(3):
                gated(n)
            split_next("in2", 11, quarters=(2,))
            split_x("y", 2, xcT[:, 0:4, :])
            gate(11)
            gated(3)
            split_next("in2", 11, quarters=(3,))
            split_x("y", 3, xcT[:, 4:8, :])

            def h2(j, i):
                b = bank_of("out2", j)
                done("out2", j, i)
                cols = bass.ds(i * 4 + 2 * j, 2)
                v.tensor_tensor(h2T[:, cols, :], tiles2(b), x2T[:, cols, :], ALU.add).then_inc(bank_free[b], 1)
                v.wait_ge(bank_free[b], evacuated("out2", j, i) + 1)
                v.sem_inc(S["h2_ready"], 1)

            v.wait_ge(S["res_ready"], 4)
            with v.Fori(0, 3) as i:
                for j in range(2):
                    split_next("out2", j, i)
                    h2(j, i)
            split_next("out2", 0, 3)
            h2(0, 3)
            last_panel("out2", 1, 3, lambda c: split_x("z3", c, h2T[:, 4 * c:4 * c + 4, :], lambda k: vec("norm2_g_2", k)), lambda: h2(1, 3))

            def token_norm(hf):
                v.wait_ge(S["rtn_ready"], hf + 1)
                do(v.reciprocal(rsn[:, hf:hf + 1], rtn[:, hf:hf + 1]))
                v.wait_ge(S["bc2_in"], 16)
                v.scalar_tensor_tensor(znat[:, hf, :], bank(2, 4), rsn[:, hf:hf + 1], g2bc, op0=ALU.mult, op1=ALU.mult)\
                    .then_inc(S["znat_ready"], 1)

            def choose(r, par, before, parts=range(4)):
                steps = [(0, 6, 11, 17)[parts[0]]]

                def step(ins):
                    steps[0] += 1
                    ins.then_inc(S["top_step"], 1)
                    v.wait_ge(S["top_step"], before + steps[0])
                    v.nop(nofuse=True)

                if 0 in parts:
                    step(v.tensor_copy(row, scores[:, bass.ds(r, 1)].rearrange("p a s k -> p (a s) k")))

                def top16(values, spare, best, at):
                    step(v.max(best[:, 0:8], values))
                    step(v.max_index(at[:, 0:8], best[:, 0:8], values))
                    step(v.match_replace(spare, best[:, 0:8], values, LOWEST))
                    step(v.max(best[:, 8:16], spare))
                    step(v.max_index(at[:, 8:16], best[:, 8:16], spare))

                for s in range(2):
                    if s in parts:
                        top16(row[:, s, :], row2[:, s, :], tv[:, s, :], ti_u[:, s, :])
                if 2 in parts:
                    step(v.tensor_tensor(cand, tv[:, 0, :].unsqueeze(2).to_broadcast([P, TOPK, TOPK]),
                                         tv[:, 1, :].unsqueeze(1).to_broadcast([P, TOPK, TOPK]), ALU.add))
                    flat, flat2 = (c.rearrange("p a b -> p (a b)") for c in (cand, cand2))
                    top16(flat, flat2, top[:, par, :], pos[:])
                    v.tensor_scalar(nm[:, par:par + 1], top[:, par, 0:1], -1.0, None, ALU.mult).then_inc(S["top_ready"], 1)
                if 3 in parts:
                    step(v.tensor_copy(ti_f[:], ti_u[:]))
                    step(v.tensor_scalar(posab[:, 0, :], pos[:], 4, None, ALU.logical_shift_right))
                    step(v.tensor_scalar(posab[:, 1, :], pos[:], 15, None, ALU.bitwise_and))
                    step(v.tensor_copy(posf[:], posab[:]))
                    for s in range(2):
                        step(v.tensor_tensor(cand, posf[:, s, :].unsqueeze(2).to_broadcast([P, TOPK, TOPK]),
                                             iota16[:].unsqueeze(1).to_broadcast([P, TOPK, TOPK]), ALU.is_equal))
                        step(v.tensor_tensor(cand, cand, ti_f[:, s, :].unsqueeze(1).to_broadcast([P, TOPK, TOPK]), ALU.mult))
                        step(v.tensor_reduce(pick[:, s, :], cand, AX.X, ALU.add))
                    step(v.scalar_tensor_tensor(expf[:], pick[:, 0, :], float(KEYS), pick[:, 1, :], op0=ALU.mult, op1=ALU.add))
                return steps[0]

            CHOOSE = 28
            for j in range(8):
                if j < 7:
                    split_next("wq", j)
                if j == 0:
                    v.wait_ge(S["rt_ready"], 3)
                    do(v.reciprocal(rstd[:], rt[:]))
                b = bank_of("wq", j)
                done("wq", j)
                v.tensor_tensor(qp[:, 2 * j:2 * j + 2, :], tiles2(b), rstd2, ALU.mult).then_inc(bank_free[b], 1)
                if j in (1, 3):
                    token_norm(j // 2)
                if j >= 1:
                    v.wait_ge(S["sc_evac"], 1 if j < 5 else 2)
                    for part in {1: (0,), 2: (1,), 3: (2,), 4: (3,), 5: (4,), 6: (5, 6), 7: (7,)}[j]:
                        r = part // 4
                        choose(r, r, CHOOSE * r, (part % 4,))
                        if part == 3:
                            do(v.tensor_copy(idx[:, r, :], expf[:]))
                            v.sem_inc(S["idx_ready"], 1)
            v.wait_ge(S["sc_zero"], 1)
            v.wait_ge(S["znat_ready"], 2)
            for hf in range(HALVES):
                with v.Fori(0, PEER_HEADS // 2) as i:
                    for par in range(2):
                        r = i * 2 + (PEER_HEADS * hf + par)
                        for k in range(TOPK):
                            s = k % 4
                            if k == TOPK - 4:
                                v.wait_ge(v_free[3], r * 4 + 1)
                                v.tensor_copy(idx[:, 1 - par, :], expf[:]).then_inc(S["idx_ready"], 1)
                                v.wait_ge(S["idx_ready"], r + 2)
                            v.wait_ge(u_landed[s], r * 64 + 16 * (k // 4 + 1))
                            if k >= 2:
                                v.wait_ge(u_free[(k - 2) % 4], r * 4 + ((k - 2) // 4 + 2))
                            v.tensor_tensor_reduce(out=junk[k % 2], in0=ubuf[s], in1=znat[:, hf, :], scale=1.0, scalar=0.0,
                                                   op0=ALU.mult, op1=ALU.add, accum_out=act[:, par, k:k + 1]).then_inc(u_free[s], 1)
                        v.wait_ge(u_free[3], r * 4 + 5)
                        v.tensor_tensor(asq[:], act[:, par, :], act[:, par, :], ALU.mult).then_inc(S["gel_step"], 1)
                        v.wait_ge(S["gel_step"], r * 3 + 1)
                        v.scalar_tensor_tensor(ain[:, par, :], asq[:], 1.0 / GELU_C, act[:, par, :], op0=ALU.add, op1=ALU.mult)\
                            .then_inc(S["inner_ready"], 1)
                        v.wait_ge(S["ex_done"], r + 1)
                        v.reciprocal(er[:, par:par + 1], es[:, par:par + 1]).then_inc(S["gel_step"], 1)
                        v.wait_ge(S["gel_step"], r * 3 + 2)
                        v.scalar_tensor_tensor(agx[:, par, :], act[:, par, :], er[:, par:par + 1], eg[:, par, :], op0=ALU.mult, op1=ALU.mult)\
                            .then_inc(S["gel_step"], 1)
                        v.wait_ge(S["gel_step"], r * 3 + 3)
                        v.wait_ge(S["gel_done"], r + 1)
                        v.scalar_tensor_tensor(wk[:, par, :], ath[:, par, :], 1.0, agx[:, par, :], op0=ALU.add, op1=ALU.mult)\
                            .then_inc(S["w_ready"], 1)
                        v.wait_ge(S["sc_evac"], PEER_HEADS)
                        choose(r + 2, par, r * CHOOSE + 2 * CHOOSE)
            for hf in range(HALVES):
                v.wait_ge(S["fin_rt"], hf + 1)
                do(v.reciprocal(rsn[:, hf:hf + 1], rtn[:, hf:hf + 1]))
                v.wait_ge(S["bcf_in"], 16)
                v.scalar_tensor_tensor(stage[:, hf, :], bank(4 * hf, 4), rsn[:, hf:hf + 1], gfbc, op0=ALU.mult, op1=ALU.mult)\
                    .then_inc(S["fin_out"], 1)

        @block.tensor
        def _(pe):
            mm, tr = nc.tensor.matmul, nc.tensor.transpose
            pe.sem_inc(S["s_free"], 1)
            pe.sem_inc(S["o_free"], 1)
            pe.sem_inc(S["pv_done"], AHEAD)

            def product(section, j, i=0, operand=None, tiles=2, outs=None):
                b = bank_of(section, j)
                if STARTS[section] + j >= 2:
                    pe.wait_ge(bank_free[b], evacuated(section, j, i))
                before = quarters_before(section, j, i)
                for q in range(QUARTERS):
                    pe.wait_ge(S["wl_ready"], before + (q + 1))
                    o = tiles2(b if outs is None else outs[q // 2])
                    first = q == 0 or (outs is not None and q == 2)
                    last = q == QUARTERS - 1 or (outs is not None and q == 1)

                    def parts(pairs, begins, ends):
                        for k in range(QUARTER_KT):
                            n = QUARTER_KT * q + k
                            for t in range(tiles):
                                c = slice(t * P, (t + 1) * P)
                                for m, (w, x) in enumerate(pairs):
                                    ins = mm(o[:, t, :], w[:, q, k, c], x[:, n, :], start=(begins and k == t == m == 0),
                                             stop=(ends and k == QUARTER_KT - 1 and m == len(pairs) - 1), skip_group_check=True)
                        return ins

                    if operand is None:
                        ins = parts(((WH, XH), (WH, XL), (WL, XH)), first, last)
                    else:
                        pe.wait_ge(S["xh_ready"], 4 * STAGES[operand] + q + 1)
                        parts(((WH, XH), (WL, XH)), first, False)
                        pe.wait_ge(S["x_ready"], 4 * STAGES[operand] + q + 1)
                        ins = parts(((WH, XL),), False, last)
                    ins.then_inc(S["w_used"], 1)

            def mean_square(n, halves):
                pe.wait_ge(S["sum_ready"], n + 1)
                for m in range(halves):
                    for t in range(2):
                        ins = mm(bank(7)[:, m * TOK:(m + 1) * TOK], ones[:], acc[:, m, t, :], start=(t == 0), stop=(t == 1), skip_group_check=True)
                ins.then_inc(S["ss_done"], 1)

            pe.wait_ge(S["ident_ready"], 1)
            pe.wait_ge(S["vec_in"], 16 * (len(VEC_A) + len(VEC_B) + 2))
            tr(bank(0)[:, 0:P], vecA, ident[:])
            tr(bank(0)[:, P:VEC_COLS], vecB, ident[0:VEC_B_ROWS, 0:VEC_B_ROWS]).then_inc(S["vec_t"], 1)
            pe.wait_ge(S["xn_ready"], HALVES)
            for c in range(4):
                if c == 3:
                    pe.wait_ge(S["x_ready"], 1)
                for k in range(4):
                    for h in range(HALVES):
                        ins = tr(bank(2 + 2 * (c % 3), 2)[:, k * TOK + h * P:k * TOK + (h + 1) * P], xnat0[:, h, (4 * c + k) * P:(4 * c + k + 1) * P], ident[:])
                ins.then_inc(S["xt_done"], 1)
            pe.wait_ge(S["vecs_ready"], 1)
            for j in range(4):
                product("q", j, operand="h" if j == 0 else None)
            product("gl", 0, tiles=1)
            for j in range(6):
                product("kv", j)
                if j == 0:
                    pe.wait_ge(S["gl_ready"], 1)
                    for h in range(HALVES):
                        ins = tr(bank(7)[:, h * 64:h * 64 + 3 * HEADS], glT[:, h * P:(h + 1) * P], ident[0:3 * HEADS, 0:3 * HEADS])
                    ins.then_inc(S["gl_t"], 1)
                if j == 3:
                    pe.wait_ge(S["cmp_in"], 16 * 8)
                    pe.wait_ge(S["kab_ready"], 4)
                    for s in range(2):
                        for l in range(CMP_LEN):
                            part, at = l // CMP_STRIDE, l % CMP_STRIDE
                            rhs = kab[:, 2 * s + part].rearrange("p t (n l) -> p t n l", l=CMP_STRIDE)[:, :, part:part + NC_BLOCKS, at]
                            ins = mm(bank(2 + s)[:, 0:2 * NC_BLOCKS], w1bd[:, s, l, :], rhs, start=(l == 0), stop=(l == CMP_LEN - 1))
                        ins.then_inc(S["hid_done"], 1)
                if j == 4:
                    pe.wait_ge(S["hid_ready"], 2)
                    mm(bank(4)[:, 0:2 * NC_BLOCKS], w2bd[:, 0, :], hid[:, 0, :], start=True, stop=True).then_inc(S["kc_done"], 1)
                    for t in range(2):
                        ins = mm(bank(5)[0:NC_BLOCKS, t * P:(t + 1) * P], hid[:, 1, t * NC_BLOCKS:(t + 1) * NC_BLOCKS], w2bd[:, 1, :], start=True, stop=True)
                    ins.then_inc(S["kc_done"], 1)

            def values(typ, which):
                pe.wait_ge(S["kv_evac"], which + 1)
                for kt in range(2):
                    for t in range(2):
                        at = kt * TOK + t * P
                        ins = tr(bank(2 + typ)[:, at:at + P], kvT[:, which, t, kt * P:(kt + 1) * P], ident[:])
                ins.then_inc(S["vt_done"], 1)

            def keys_twice(typ, which):
                for t in range(2):
                    for s in range(2):
                        ins = mm(tiles2(4 + 2 * typ + t)[:, s, :], dup[:, s, :], kvT[:, which, t, :], start=True, stop=True)
                    ins.then_inc(S["dup_done"], 1)

            values(0, 3)
            pe.wait_ge(S["dist_ready"], 1)
            pe.wait_ge(S["kc_ready"], 1)
            for t in range(2):
                for s in range(2):
                    g = 2 * t + s
                    ins = mm(bank(6)[:, g * NCP:(g + 1) * NCP], dup[:, s, :], kcT[:, t, :], start=True, stop=True)
            ins.then_inc(S["kcdup_done"], 1)
            pe.wait_ge(S["vall_ready"], 1)
            keys_twice(0, 2)
            pe.wait_ge(S["gates_ready"], 6)
            pe.wait_ge(S["kcpad_ready"], 2)
            keys_twice(1, 4)
            values(1, 5)

            with pe.Fori(0, GROUPS) as i:
                def head_scores(h):
                    pr, par = h // 2, h % 2
                    if h == 0:
                        pe.wait_ge(S["qv_ready"], i + 1)
                    pe.wait_ge(S["s_free"], i * 4 + (h + 1))
                    q0, q1 = qcur[:, pr, 0:P], qcur[:, pr, P:TOK]
                    mm(pS[:, 0:512], q1, kpad[:, par, :, bass.ds(i, 1), :].rearrange("p t g n -> p (t g) n"), start=True, stop=True)
                    mm(pS[:, 512:768], q0, kpad[:, par, :, bass.ds(i, 1), 0:P].rearrange("p t g n -> p (t g) n"), start=True, stop=True)
                    kc = kcpad[:, par, bass.ds(i, 1), :].rearrange("p g n -> p (g n)")
                    mm(pS[:, 768:784], q0, kc, start=True, stop=True)
                    mm(pS[:, 784:800], q1, kc, start=True, stop=True).then_inc(S["s_done"], 1)

                def head_turn(h):
                    pe.wait_ge(S["e_ready"], i * 4 + (h + 1))
                    for at, src in ((0, 512), (P, 0), (2 * P, 640), (3 * P, TOK), (4 * P, P), (5 * P, TOK + P)):
                        tr(pT_[:, at:at + P], eT[:, src:src + P], ident[:])
                    tr(pT_[0:NCP, 768:896], eT[:, 768:784], ident[:])
                    tr(pT_[0:NCP, 896:1024], eT[:, 784:800], ident[:]).then_inc(S["pt_done"], 1)

                def head_values(h):
                    par = h % 2
                    pe.wait_ge(S["pts_ready"], i * 4 + (h + 1))
                    if par == 0:
                        pe.wait_ge(S["o_free"], i * 2 + (h // 2 + 1))
                    cols = slice(0, P) if par else slice(HD, 3 * HD)
                    for n, (at, size, src) in enumerate(((0, TOK, 0), (P, P, 512), (0, TOK, TOK), (P, P, 640))):
                        mm(pO[:, at:at + size], vcur[:, n, cols], pts[:, src:src + size], start=(par == 0 and n == 0), stop=False,
                           skip_group_check=True)
                    mm(pO, vcur[0:NCP, 4, cols], pts[0:NCP, 768:1024], start=False, stop=(par == 1), skip_group_check=True)\
                        .then_inc(S["pv_done"], 1)

                for j in range(6):
                    product("main", j, i)
                    if 2 <= j <= 5:
                        head_values(j - 2)
                    if 1 <= j <= 4:
                        head_turn(j - 1)
                    if j <= 3:
                        head_scores(j)

            def spatial(step):
                if step == 0:
                    j = 2
                    pe.wait_ge(bank_free[bank_of("main", j)], evacuated("main", j, GROUPS - 1) + 1)
                    pe.wait_ge(S["s_free"], HEADS + 1)
                    for k in range(BT):
                        ins = mm(bank(2)[:, 0:TOK], ones[:], vT[:, k, :], start=(k == 0), stop=(k == BT - 1))
                    ins.then_inc(S["mean_done"], 1)
                if step == 2:
                    pe.wait_ge(S["vsq_ready"], 1)
                    for k in range(BT):
                        ins = mm(bank(3)[:, 0:TOK], ones[:], vsq[:, k, :], start=(k == 0), stop=(k == BT - 1))
                    ins.then_inc(S["var_done"], 1)
                    pe.wait_ge(S["sgu_in"], 32)
                    for n in range(2):
                        for g in range(4):
                            ins = tr(bank(4 + n)[:, g * P:(g + 1) * P], sgun[:, 4 * n + g, :], ident[:])
                        ins.then_inc(S["sgu_t"], 1)
                if step == 4:
                    pe.wait_ge(S["sgu_t_evac"], 2)
                    pe.wait_ge(S["y_ready"], BT)
                    pe.wait_ge(S["o_free"], 2 * GROUPS + 1)
                    for n in range(4):
                        c, g0 = n // 2, 4 * (n % 2)
                        for g in range(4):
                            ins = tr(bank(4 + n)[:, g * P:(g + 1) * P], vT[:, g0 + g, c * P:(c + 1) * P], ident[:])
                        ins.then_inc(S["yt_done"], 1)
                if step == 6:
                    pe.wait_ge(S["wt_ready"], 1)
                    pe.wait_ge(S["vn_ready"], 4)
                    for n in range(4):
                        for t in range(2):
                            g = 2 * n + t
                            for c in range(HALVES):
                                o = tiles2(4 + n)[:, t, c * P:(c + 1) * P]
                                mm(o, vn[:, c, g, :], sguT[:, g, :], start=True, stop=False)
                                ins = mm(o, ones[0:1, :], sgub[0:1, g * P:(g + 1) * P], start=False, stop=True)
                        ins.then_inc(S["sv_done"], 1)

            for j in range(8):
                spatial(j)
                product("merge", j)
            with pe.Fori(0, 4) as i:
                for j in range(2):
                    b = bank_of("up", j)
                    product("up", j, i, operand="branches", outs=(b, 2 + b))
            def turn_x(n):
                if n >= 4:
                    pe.wait_ge(S["xt2_ready"], n - 3)
                for t in range(2):
                    for h in range(HALVES):
                        ins = tr(tiles2(4 + n % 4)[:, t, h * P:(h + 1) * P], xnat1[:, h, (2 * n + t) * P:(2 * n + t + 1) * P], ident[:])
                ins.then_inc(S["xt2_done"], 1)

            pe.wait_ge(S["xnat_in"], 16 * HALVES)
            for n in range(4):
                turn_x(n)
            product("out", 0, 0, operand="merged")
            for n in range(4, 8):
                turn_x(n)
            product("out", 1, 0)
            with pe.Fori(1, 4) as i:
                for j in range(2):
                    product("out", j, i)
            pe.wait_ge(S["pnat_in"], 16)
            pe.wait_ge(S["xt2_ready"], 8)
            for t in range(2):
                for h in range(HALVES):
                    ins = tr(tiles2(4)[:, t, h * P:(h + 1) * P], pnat[:, h, t * P:(t + 1) * P], ident[:])
            ins.then_inc(S["pt_t"], 1)
            pe.wait_ge(S["wple_in"], 16)
            for j in range(8):
                b = bank_of("ple", j)
                product("ple", j, operand="x1" if j == 0 else None)
                if j == 0:
                    pe.wait_ge(S["pt_ready"], 1)
                for t in range(2):
                    for k in range(2):
                        at = j * PANEL + t * P
                        ins = mm(tiles2(2 + b)[:, t, :], wple[:, k, at:at + P], pT[:, k, :], start=(k == 0), stop=(k == 1))
                ins.then_inc(S["pg_done"], 1)
            for j in range(12):
                product("in2", j, operand="z2" if j == 0 else None)
                if j == 0:
                    mean_square(0, 2)
                if j == 6:
                    pe.wait_ge(S["blk2_in"], 48)
                    for h in range(BT):
                        pe.wait_ge(S["xc2_ready"], h + 1)
                        if h >= 4:
                            pe.wait_ge(S["gate_evac"], 2 * (h - 3))
                        mm(bank(2 + h % 4)[:, 0:TOK], gaw[:, h, :], xcT[:, h, :], start=True, stop=True)
                        mm(bank(2 + h % 4)[:, TOK:2 * TOK], gxw[:, h, :], xcT[:, h, :], start=True, stop=True).then_inc(S["gate_mm"], 1)
                if j == 9:
                    pe.wait_ge(S["gate_evac"], 2 * BT)
                    for n in range(4):
                        pe.wait_ge(S["pooled"], n + 1)
                        for t in range(2):
                            for k in range(2):
                                ins = mm(tiles2(2 + n)[:, t, :], poolw[:, n, k, t * P:(t + 1) * P], upad[:, 2 * n + k, PAD:PAD + TOK], start=(k == 0), stop=(k == 1))
                        ins.then_inc(S["pool_mm"], 1)
            with pe.Fori(0, 4) as i:
                for j in range(2):
                    product("out2", j, i, operand="y")
            pe.wait_ge(S["keys_in"], 32)
            for n in range(4):
                for g in range(4):
                    ins = tr(bank(4 + n)[:, g * P:(g + 1) * P], keysn[:, n // 2, 4 * (n % 2) + g, :], ident[:])
                ins.then_inc(S["keys_t"], 1)

            def token_order(hf, b):
                for k in range(KT):
                    ins = mm(bank(b + k // 4)[:, (k % 4) * P:(k % 4 + 1) * P], h2T[:, k, hf * P:(hf + 1) * P], ident[:],
                             start=(k % 4 == 0), stop=True, skip_group_check=True)
                return ins

            def key_scores(h):
                pe.wait_ge(bank_free[bank_of("wq", h)], evacuated("wq", h) + 1)
                if h == 1:
                    pe.wait_ge(S["rt_ready"], 3)
                if h >= 2:
                    pe.wait_ge(S["sc_evac"], h - 1)
                for hf in range(HALVES):
                    for s in range(2):
                        ins = mm(tiles2(6 + h % 2)[:, hf, s * KEYS:(s + 1) * KEYS], qp[:, 2 * h + s, hf * P:(hf + 1) * P], keysT[:, s, h, :],
                                 start=True, stop=True, skip_group_check=True)
                ins.then_inc(S["sc_done"], 1)

            for j in range(8):
                product("wq", j, operand="z3" if j == 0 else None)
                if j == 0:
                    pe.wait_ge(S["keys_evac"], 4)
                    mean_square(1, 1)
                    pe.wait_ge(S["h2_ready"], 8)
                    token_order(0, 2).then_inc(S["h2t_done"], 1)
                if j == 2:
                    pe.wait_ge(S["znat_ready"], 1)
                    token_order(1, 2).then_inc(S["h2t_done"], 1)
                if j:
                    key_scores(j - 1)
            key_scores(7)
            pe.wait_ge(S["sc_evac"], PEER_HEADS)
            pe.wait_ge(S["znat_ready"], HALVES)
            for hf in range(HALVES):
                token_order(hf, 4 * hf)
            for hf in range(HALVES):
                with pe.Fori(0, PEER_HEADS // 2) as i:
                    for par in range(2):
                        r = i * 2 + (PEER_HEADS * hf + par)
                        for k in range(TOPK):
                            s = k % 4
                            pe.wait_ge(diag_ready[s], r * 4 + (k // 4 + 1))
                            pe.wait_ge(v_landed[s], r * 64 + 16 * (k // 4 + 1))
                            for c in range(4):
                                ins = mm(bank(4 * hf + c), diag[:, s, :], vbuf[s][:, 512 * c:512 * (c + 1)], start=False, stop=True,
                                         skip_group_check=True)
                            ins.then_inc(v_free[s], 1)


_INS = ["x", "p", "norm_g", "w_in", "cmp_pe_k", "cmp_w1_k", "cmp_w2_k", "cmp_pe_v", "cmp_w1_v", "cmp_w2_v", "ln_v_g",
        "ln_v_b", "sgu_w", "sgu_b", "w_up_a", "w_up_b", "w_out", "w_ple", "w_ple_gate", "final_g", "norm1_g_2", "w_in_2",
        "pool_w_2", "pool_b_2", "pool_scale_2", "conv_w_2", "conv_b_2", "gate_a_w_2", "gate_a_b_2", "gate_x_w_2",
        "gate_x_b_2", "lru_lambda_2", "w_out_2", "norm2_g_2", "peer_wq_2", "peer_keys1_2", "peer_keys2_2", "peer_u_2",
        "peer_v_2", "norm_f_g_2"]


def kernel(**inputs):
    import concourse.bacc as bacc
    from concourse.bass_utils import run_bass_kernel_spmd

    nc = bacc.Bacc("TRN2", target_bir_lowering=False, num_devices=1)
    arrays, aps = {}, {}
    for name in _INS:
        a = np.ascontiguousarray(inputs[name])
        arrays[f"in_{name}"] = a
        aps[name] = nc.dram_tensor(f"in_{name}", a.shape, mybir.dt.from_np(a.dtype), kind="ExternalInput").ap()
    out = nc.dram_tensor("out", (1, TOK, D), mybir.dt.float32, kind="ExternalOutput").ap()
    build(nc, aps, out)
    result = run_bass_kernel_spmd(nc, [arrays], core_ids=[0])
    return result.results[0]["out"]
```
